# Optimizing a Trainium2 kernel written in Bass

```python
import math
import jax, jax.numpy as jnp
from jax import lax
import numpy as np

D_MODEL = 1024
BATCH = 1
SEQ = 256
DEPTH = 1

POOL_WIDTH = D_MODEL // 2
POOL_WINDOWS = (2, 4, 8, 16)
N_POOL_GROUPS = 4
POOL_GROUP = POOL_WIDTH // N_POOL_GROUPS
HEAD_DIM = 64
N_Q_HEADS = (D_MODEL // 2) // HEAD_DIM
N_KV_HEADS = N_Q_HEADS // 4
Q_PER_KV = N_Q_HEADS // N_KV_HEADS
ATTN_WIDTH = N_Q_HEADS * HEAD_DIM
KV_WIDTH = N_KV_HEADS * HEAD_DIM
WINDOW = 128
BLOCK = 128
N_BUCKETS = 32
MAX_DISTANCE = 128
N_EXPERTS = 32
TOP_K = 4
D_FF = D_MODEL
SWIGLU_LIMIT = 7.0
SWIGLU_ALPHA = 1.702
RMS_EPS = 1e-5
IN_WIDTH = POOL_WIDTH + ATTN_WIDTH + 2 * KV_WIDTH + 2 * D_MODEL
SPLITS = (POOL_WIDTH,
          POOL_WIDTH + ATTN_WIDTH,
          POOL_WIDTH + ATTN_WIDTH + KV_WIDTH,
          POOL_WIDTH + ATTN_WIDTH + 2 * KV_WIDTH,
          POOL_WIDTH + ATTN_WIDTH + 2 * KV_WIDTH + D_MODEL)

kernel_name = "hybrid_pool_swa_sink_moe"

def rmsnorm(x, g):
    xf = x.astype(jnp.float32)
    y = xf * lax.rsqrt(jnp.mean(xf * xf, axis=-1, keepdims=True) + RMS_EPS)
    return (y * g.astype(jnp.float32)).astype(x.dtype)

def t5_bucket(dist):
    max_exact = N_BUCKETS // 2
    d = np.maximum(dist, 1).astype(np.float32)
    large = max_exact + (np.log(d / max_exact) / math.log(MAX_DISTANCE / max_exact)
                         * (N_BUCKETS - max_exact)).astype(np.int32)
    large = np.minimum(large, N_BUCKETS - 1)
    return np.where(dist < max_exact, dist, large).astype(np.int32)

def multiscale_pool(u, pool_w, pool_scale):
    B, S, _ = u.shape
    ug = u.reshape(B, S, N_POOL_GROUPS, POOL_GROUP).astype(jnp.float32)
    cs = jnp.cumsum(ug, axis=1)
    cs0 = jnp.pad(cs, ((0, 0), (1, 0), (0, 0), (0, 0)))
    pos = jnp.arange(1, S + 1, dtype=jnp.float32)
    means = []
    for g, w in enumerate(POOL_WINDOWS):
        lo = jnp.pad(cs0[:, :S + 1 - w, g], ((0, 0), (w - 1, 0), (0, 0)))
        cnt = jnp.minimum(pos, float(w))[None, :, None]
        means.append((cs[:, :, g] - lo) / cnt)
    z = (jnp.stack(means, axis=2) - ug).astype(u.dtype)
    z = jnp.einsum('bsgc,gcd->bsgd', z, pool_w)
    return z.reshape(B, S, POOL_WIDTH) * pool_scale

def sliding_window_attention(q, k, v, sinks, rel_bias):
    B, S, _ = q.shape
    nb = S // BLOCK
    qb = q.reshape(B, nb, BLOCK, N_KV_HEADS, Q_PER_KV, HEAD_DIM)
    k4 = k.reshape(B, S, N_KV_HEADS, HEAD_DIM)
    v4 = v.reshape(B, S, N_KV_HEADS, HEAD_DIM)
    pad = ((0, 0), (BLOCK, 0), (0, 0), (0, 0))
    kp, vp = jnp.pad(k4, pad), jnp.pad(v4, pad)
    blk = (B, nb, BLOCK, N_KV_HEADS, HEAD_DIM)
    kb = jnp.concatenate([kp[:, :S].reshape(blk), k4.reshape(blk)], axis=2)
    vb = jnp.concatenate([vp[:, :S].reshape(blk), v4.reshape(blk)], axis=2)

    qi = np.arange(BLOCK)[:, None]
    kj = np.arange(2 * BLOCK)[None, :]
    dist = BLOCK + qi - kj
    in_band = (dist >= 0) & (dist < WINDOW)
    bucket = t5_bucket(np.clip(dist, 0, None))
    bias = jnp.transpose(rel_bias[bucket].astype(jnp.float32), (2, 0, 1))
    bias = bias.reshape(N_KV_HEADS, Q_PER_KV, BLOCK, 2 * BLOCK)
    kpos = (np.arange(nb)[:, None, None] - 1) * BLOCK + kj[None]
    mask = in_band[None] & (kpos >= 0)

    scores = jnp.einsum('bnqhgd,bnkhd->bnhgqk', qb, kb,
                        preferred_element_type=jnp.float32) * (HEAD_DIM ** -0.5)
    scores = jnp.where(mask[None, :, None, None], scores + bias[None, None], -1e30)
    sink = jnp.broadcast_to(sinks.astype(jnp.float32).reshape(1, 1, N_KV_HEADS, Q_PER_KV, 1, 1),
                            scores.shape[:-1] + (1,))
    probs = jax.nn.softmax(jnp.concatenate([scores, sink], axis=-1), axis=-1)[..., :-1]
    out = jnp.einsum('bnhgqk,bnkhd->bnqhgd', probs.astype(v.dtype), vb)
    return out.reshape(B, S, ATTN_WIDTH)

def clamped_swiglu(hu):
    glu, lin = hu[..., ::2], hu[..., 1::2]
    glu = jnp.minimum(glu, SWIGLU_LIMIT)
    lin = jnp.clip(lin, -SWIGLU_LIMIT, SWIGLU_LIMIT)
    return glu * jax.nn.sigmoid(SWIGLU_ALPHA * glu) * (lin + 1.0)

def moe(h, w_router, b_router, w_up, b_up, w_down, b_down):
    B, S, D = h.shape
    t = h.reshape(-1, D)
    logits = (t @ w_router + b_router).astype(jnp.float32)
    top_vals, top_idx = lax.top_k(logits, TOP_K)
    top_w = jax.nn.softmax(top_vals, axis=-1)
    gates = jnp.einsum('tk,tke->te', top_w, jax.nn.one_hot(top_idx, N_EXPERTS, dtype=jnp.float32))
    out = jnp.zeros((t.shape[0], D), jnp.float32)
    for e in range(N_EXPERTS):
        act = clamped_swiglu(t @ w_up[e] + b_up[e])
        out = out + gates[:, e:e + 1] * (act @ w_down[e] + b_down[e]).astype(jnp.float32)
    return out.astype(h.dtype).reshape(B, S, D)

def setup_inputs(seed: int = 0) -> dict:
    key = jax.random.key(seed)
    ks = jax.random.split(key, 20)
    f32 = jnp.float32
    n = lambda k, shape, s: jax.random.normal(k, shape, f32) * s
    return {
        "x": n(ks[0], (BATCH, SEQ, D_MODEL), 1.0),
        "norm1_g": 1.0 + n(ks[1], (DEPTH, D_MODEL), 0.02),
        "w_in": n(ks[2], (DEPTH, D_MODEL, IN_WIDTH), D_MODEL ** -0.5),
        "pool_w": n(ks[3], (DEPTH, N_POOL_GROUPS, POOL_GROUP, POOL_GROUP), POOL_GROUP ** -0.5),
        "pool_scale": 1.0 + n(ks[4], (DEPTH, POOL_WIDTH), 0.02),
        "w_pool_proj": n(ks[5], (DEPTH, POOL_WIDTH, D_MODEL), POOL_WIDTH ** -0.5),
        "sinks": n(ks[6], (DEPTH, N_Q_HEADS), 1.0),
        "w_attn_proj": n(ks[7], (DEPTH, ATTN_WIDTH, D_MODEL), ATTN_WIDTH ** -0.5),
        "w_out": n(ks[8], (DEPTH, D_MODEL, D_MODEL), D_MODEL ** -0.5),
        "norm2_g": 1.0 + n(ks[9], (DEPTH, D_MODEL), 0.02),
        "w_router": n(ks[10], (DEPTH, D_MODEL, N_EXPERTS), D_MODEL ** -0.5),
        "b_router": n(ks[11], (DEPTH, N_EXPERTS), 0.01),
        "w_up": n(ks[12], (DEPTH, N_EXPERTS, D_MODEL, 2 * D_FF), D_MODEL ** -0.5),
        "b_up": n(ks[13], (DEPTH, N_EXPERTS, 2 * D_FF), 0.01),
        "w_down": n(ks[14], (DEPTH, N_EXPERTS, D_FF, D_MODEL), D_FF ** -0.5),
        "b_down": n(ks[15], (DEPTH, N_EXPERTS, D_MODEL), 0.01),
        "rel_bias": n(ks[16], (N_BUCKETS, N_Q_HEADS), 0.5),
        "final_g": 1.0 + n(ks[17], (D_MODEL,), 0.02),
    }

def reference(x, norm1_g, w_in, pool_w, pool_scale, w_pool_proj, sinks, w_attn_proj, w_out,
              norm2_g, w_router, b_router, w_up, b_up, w_down, b_down, rel_bias, final_g):
    for l in range(DEPTH):
        h = rmsnorm(x, norm1_g[l])
        u, q, k, v, g_pool, g_attn = jnp.split(h @ w_in[l], SPLITS, axis=-1)
        y_pool = multiscale_pool(u, pool_w[l], pool_scale[l]) @ w_pool_proj[l]
        y_attn = sliding_window_attention(q, k, v, sinks[l], rel_bias) @ w_attn_proj[l]
        mixed = jax.nn.sigmoid(g_pool) * y_pool + jax.nn.sigmoid(g_attn) * y_attn
        x = x + mixed @ w_out[l]
        x = x + moe(rmsnorm(x, norm2_g[l]), w_router[l], b_router[l], w_up[l], b_up[l],
                    w_down[l], b_down[l])
    return rmsnorm(x, final_g)


_drawn_inputs = setup_inputs


def setup_inputs(seed=0):
    import zlib

    import numpy as np

    out = dict(_drawn_inputs(seed))
    spreads = {}
    factors = {'sinks': 2.829, 'b_up': 8.0, 'b_down': 8.0, 'final_g': 2.871}
    for name, (base, spread) in spreads.items():
        noise = np.random.default_rng([zlib.crc32(name.encode()), seed]).standard_normal(out[name].shape)
        drawn = base * np.exp(spread * noise) if base else spread * noise
        out[name] = __import__('jax').numpy.asarray(drawn.astype(out[name].dtype))
    for name, factor in factors.items():
        out[name] = (out[name] * factor).astype(out[name].dtype)
    return out
```

```python
import math
from contextlib import ExitStack

import numpy as np

import concourse.bass as bass
from concourse import mybir

F32 = mybir.dt.float32
I32 = mybir.dt.int32
ALU = mybir.AluOpType
ACT = mybir.ActivationFunctionType
AX = mybir.AxisListType

P = 128
D = 1024
SEQ = 256
TT = SEQ // P
KD = D // P
POOL_WIDTH = 512
POOL_WINDOWS = (2, 4, 8, 16)
NG = len(POOL_WINDOWS)
PAD = max(POOL_WINDOWS)
HEADS, KV_HEADS, HD = 8, 2, 64
ATTN_WIDTH = HEADS * HD
KW = ATTN_WIDTH // P
WINDOW = 128
N_BUCKETS, MAX_DISTANCE = 32, 128
MASKED = -1e30
E, TOP_K = 32, 4
LIMIT, ALPHA, EPS = 7.0, 1.702, 1e-5

SLOTS = P // 2
PASSES = E // 2
ROUNDS = SEQ // SLOTS - 1
LISTED = 16
NJ, CH = 4, 512
CF = CH // 2
UNRANKED = 1024.0

R = 10
SLOT = KD * CH
C_Q, C_KV, C_U, C_GP, W_POOL, C_GPA, W_ATTN, C_GA, C_GA2, W_OUT0, W_OUT1 = range(11)
MIXER_LOADS = 11
W_IN_LOAD = [C_U, C_Q, C_KV, C_GP, C_GPA, C_GA, C_GA2]
GATE_POOL_AT = POOL_WIDTH + ATTN_WIDTH + 2 * KV_HEADS * HD
GATE_ATTN_AT = GATE_POOL_AT + D
LOADS = 12
UNROLL = 5
ALL_LOADS = MIXER_LOADS + PASSES * LOADS

UNITS = ([("vectors", "dve"), ("bias_rows", "dve")]
         + [(f"xT{m}", "dve") for m in range(4)]
         + [("q0", "act"), ("q1", "act"), ("kv", "dve"), ("u0", "dve"), ("u1", "dve")]
         + [(f"scores1_{i}", "dve") for i in range(4)] + [(f"scores0_{i}", "dve") for i in range(2)]
         + [("pool0", "act"), ("pool1", "act")]
         + [(f"gate_pool{c}", "dve") for c in range(KD)]
         + [(f"probsT{i}", "act" if i % 2 else "dve") for i in range(6)]
         + [("attn0", "dve"), ("attn1", "dve")]
         + [(f"gate_attn{c}", "dve") for c in range(KD)]
         + [(f"out{q}", "dve") for q in range(4)]
         + [(f"h2T{q}", "dve") for q in range(4)]
         + [("logits0", "dve"), ("logits1", "dve"), ("ranks", "dve"), ("gatesT", "act")])
UNIT = {name: n for n, (name, _) in enumerate(UNITS)}


def t5_bucket(dist):
    max_exact = N_BUCKETS // 2
    d = np.maximum(dist, 1).astype(np.float32)
    large = max_exact + (np.log(d / max_exact) / math.log(MAX_DISTANCE / max_exact)
                         * (N_BUCKETS - max_exact)).astype(np.int32)
    large = np.minimum(large, N_BUCKETS - 1)
    return np.where(dist < max_exact, dist, large).astype(np.int32)


def bucket_map():
    dist = 2 * WINDOW - 1 - np.arange(3 * WINDOW)
    inside = (dist >= 0) & (dist < WINDOW)
    rows = np.zeros((N_BUCKETS + 1, 3 * WINDOW), np.float32)
    rows[t5_bucket(np.clip(dist, 0, None))[inside], np.flatnonzero(inside)] = 1.0
    rows[N_BUCKETS, ~inside] = MASKED
    return rows


def hybrid_block_kernel(nc, x, norm1_g, w_in, pool_w, pool_scale, w_pool_proj, sinks, w_attn_proj,
                        w_out, norm2_g, w_router, b_router, w_up, b_up, w_down, b_down, rel_bias,
                        final_g, buckets, out):
    x_d = x.rearrange("b (t p) d -> (b t) p d", p=P)
    out_d = out.rearrange("b (t p) d -> (b t) p d", p=P)
    w_in_d, w_up_d, w_down_d = w_in[0], w_up[0], w_down[0]
    b_up_d = b_up[0].rearrange("e (j n) -> (e j) n", n=CH)
    skew = nc.dram_tensor("skew", [P, HEADS, 3 * WINDOW], F32, kind="Internal").ap()

    with ExitStack() as ctx:
        def sb(name, shape, dt=F32):
            return ctx.enter_context(nc.sbuf_tensor(name, shape, dt))

        def sem(name):
            return ctx.enter_context(nc.semaphore(name))

        ring = sb("ring", [P, R, SLOT])
        bank = [ctx.enter_context(nc.psum_tensor(f"bank{i}", [P, CH], F32)) for i in range(8)]

        acc = sb("acc", [P, TT, D])
        h_buf = sb("h_buf", [P, 2 * D])
        hT = h_buf[:, :].rearrange("p (k t) -> p k t", k=KD)
        x1r = h_buf[:, :].rearrange("p (t d) -> p t d", t=TT)
        m_buf = sb("m_buf", [P, 2 * D])
        xr = m_buf[:, :].rearrange("p (t d) -> p t d", t=TT)
        mixedT = m_buf[:, :].rearrange("p (k t) -> p k t", k=KD)
        hid = m_buf[:, 0:D]
        hidT = m_buf[:, D:2 * D].rearrange("p (k s) -> p k s", k=KD)
        route = m_buf[:, 0:8 * TT * E].rearrange("p (n t e) -> p n t e", n=8, t=TT)
        logits, above, equal, count_eq, chosen, expd, dist_max = (route[:, n] for n in range(7))
        gatesT = m_buf[0:E, D:D + SEQ]
        u_buf = sb("u_buf", [P, NG * (PAD + SEQ)])
        uT = u_buf[:, :].rearrange("p (g t) -> p g t", g=NG)
        pooledT = u_buf[:, 0:NG * SEQ].rearrange("p (g t) -> p g t", g=NG)
        pick = u_buf[:, 0:2 * P].rearrange("p (t s) -> p t s", t=TT)
        spread = u_buf[:, 2 * P:4 * P].rearrange("p (t s) -> p t s", t=TT)
        spreadT = u_buf[:, 4 * P:6 * P]
        extra = u_buf[:, 6 * P:6 * P + 320]
        z_buf = sb("z_buf", [P, D])
        zT = z_buf[:, :].rearrange("p (g t) -> p g t", g=NG)
        attnT = z_buf[:, :].rearrange("p (k t) -> p k t", k=KW)
        xgT = z_buf[:, :].rearrange("p (k s) -> p k s", k=KD)
        vectors = z_buf[0:2 * KD + KW, 0:P]
        h2T = [b[:, 0:D].rearrange("p (k t) -> p k t", k=KD) for b in (u_buf, z_buf)]
        y = sb("y", [P, D])
        bdn = y[0:E, :]
        swi = sb("swi", [P, 3 * CF])
        glu, lin, sig = (swi[:, n * CF:(n + 1) * CF] for n in range(3))
        bmap = swi[0:N_BUCKETS + 1, 0:3 * WINDOW]
        pw_buf = sb("pw_buf", [P, NG * P])
        pwt = pw_buf[:, :].rearrange("p (g d) -> p g d", g=NG)
        bup = pw_buf[:, 0:CH]
        row_buf = sb("row_buf", [P, NJ * P])
        ones, before = row_buf[:, 0:P], row_buf[:, P:2 * P]
        rows = row_buf[:, :].rearrange("p (j e s) -> p j e s", j=NJ, e=2)
        ident = sb("ident", [P, P])
        ids0 = sb("ids0", [P, SLOTS])
        ids = sb("ids", [P, SLOTS])
        ids_i = ids[:, :].bitcast(I32)
        w_rt = sb("w_rt", [P, KD, E])
        b_rt = sb("b_rt", [P, E])
        small = sb("small", [P, 128])
        vecT = small[:, 0:2 * KD + KW]
        g1, g2, psc = vecT[:, 0:KD], vecT[:, KD:2 * KD], vecT[:, 2 * KD:2 * KD + KW]
        ss, std, rstd = (small[:, 20 + 2 * n:22 + 2 * n] for n in range(3))
        eps, warm = small[:, 26:27], small[:, 27:28]
        snk = small[:, 28:36]
        inv_cnt = sb("inv_cnt", [P, NG, PAD])
        head = sb("head", [P, NG, PAD])
        stat = sb("stat", [P, 5, 2, HEADS])
        rank = sb("rank", [P, TT, E])
        gate = sb("gate", [P, TT, E])
        served = sb("served", [P, E])
        top = sb("top", [P, TT, 8])
        more = small[:, 36:36 + TT]
        most = small[:, 38:38 + TT]
        gsum, ginv = small[:, 40:42], small[:, 42:44]
        rel = small[0:N_BUCKETS + 1, 44:44 + HEADS]
        x_pair = sb("x_pair", [P, LISTED], I32)
        x_off = sb("x_off", [P, LISTED])
        n_extra = sb("n_extra", [P, 1], I32)
        bias_row = y[0:HEADS, 0:3 * WINDOW]

        scores1 = ring[:, 7, 0:2048].rearrange("p (h k) -> p h k", h=HEADS)
        scores0 = ring[:, 7, 2048:3072].rearrange("p (h k) -> p h k", h=HEADS)
        band = ring[:, 8, 0:2048].rearrange("p (h k) -> p h k", h=HEADS)
        qT = ring[:, 8, 2048:3072].rearrange("p (k t) -> p k t", k=KW)
        kT = ring[:, 8, 3072:3584].rearrange("p (k t) -> p k t", k=KV_HEADS)
        vv = ring[:, 8, 3584:3840].rearrange("p (t d) -> p t d", t=TT)
        probsT1 = ring[:, 9, 0:2048].rearrange("p (h k q) -> p h k q", h=HEADS, k=2)
        probsT0 = ring[:, 9, 2048:3072].rearrange("p (h q) -> p h q", h=HEADS)
        sums = [ring[:, 9, n * 1088:(n + 1) * 1088].rearrange("p (g t) -> p g t", g=NG) for n in range(2)]
        result = x1r
        fin_slot = ALL_LOADS % R
        fin_g = ring[:, fin_slot, 0:D]

        full = [sem(f"slot{i}_full") for i in range(R)]
        x_loaded = [sem("x0_loaded"), sem("x1_loaded")]
        vec_loaded, bias_in_loaded = sem("vec_loaded"), sem("bias_in_loaded")
        pw_loaded, sinks_loaded, router_loaded = sem("pw_loaded"), sem("sinks_loaded"), sem("router_loaded")
        bup_loaded, bdn_loaded, fin_loaded = sem("bup_loaded"), sem("bdn_loaded"), sem("fin_loaded")
        skew_written, band_loaded, stored = sem("skew_written"), sem("band_loaded"), sem("stored")
        consts = sem("consts")
        unit_done = sem("unit_done")
        emptied = {"dve": sem("emptied_by_dve"), "act": sem("emptied_by_act")}
        dve_step, act_step, pool_step = sem("dve_step"), sem("act_step"), sem("pool_step")
        std_ready, rstd_ready, xr_ready = sem("std_ready"), sem("rstd_ready"), sem("xr_ready")
        summed = sem("summed")
        z_ready, negmax_ready = sem("z_ready"), sem("negmax_ready")
        exp_ready, probs_ready = sem("exp_ready"), sem("probs_ready")
        sig_ready, mixed_ready = sem("sig_ready"), sem("mixed_ready")
        centred, expd_ready = sem("centred"), sem("expd_ready")
        chosen_ready, gates_ready = sem("chosen_ready"), sem("gates_ready")
        extra_ready = sem("extra_ready")
        up_done = sem("up_done")
        glu_ready, lin_ready = sem("glu_ready"), sem("lin_ready")
        sigmoid_ready, gated_ready = sem("sigmoid_ready"), sem("gated_ready")
        hid_ready = sem("hid_ready")
        hidT_done, hidT_copied = sem("hidT_done"), sem("hidT_copied")
        down_done = sem("down_done")
        y0_copied, y1_copied = sem("y0_copied"), sem("y1_copied")
        ids_ready = sem("ids_ready")
        pick_ready, spread_ready, rows_ready = sem("pick_ready"), sem("spread_ready"), sem("rows_ready")
        gather_done, xg_copied = sem("gather_done"), sem("xg_copied")
        spreadT_done, spreadT_copied = sem("spreadT_done"), sem("spreadT_copied")
        scatter_done = sem("scatter_done")
        added = sem("added")
        result_ready = sem("result_ready")

        def emptied_at(name):
            n = UNIT[name]
            by = UNITS[n][1]
            return emptied[by], sum(b == by for _, b in UNITS[:n + 1])

        def load_at(n):
            return full[n % R], 16 * (n // R + 1)

        up_banks, down_banks, turn_banks, scatter_banks = bank[0:2], bank[2:4], bank[4:6], bank[6:8]

        block = ctx.enter_context(nc.Block())

        @block.sync
        def _(sp):
            def load_w_in(n, c):
                wide = min(CH, w_in_d.shape[1] - c * CH)
                sp.dma_start(ring[:, n % R, 0:KD * wide].rearrange("p (k n) -> p k n", k=KD),
                             w_in_d[:, c * CH:c * CH + wide].rearrange("(k p) n -> p k n", p=P)).then_inc(full[n % R], 16)

            def load_rows(n, src):
                sp.dma_start(ring[:, n % R, :].rearrange("p (k n) -> p k n", n=D),
                             src.rearrange("(k p) n -> p k n", p=P)).then_inc(full[n % R], 16)

            def load_expert(slot, load, expert):
                which = expert + load % 2
                if load < 2 * NJ:
                    j = load // 2
                    src = w_up_d[bass.ds(which, 1), :, j * CH:(j + 1) * CH]
                    dst = ring[:, slot, :].rearrange("p (k n) -> p k n", n=CH)
                else:
                    half = (load - 2 * NJ) // 2
                    src = w_down_d[bass.ds(which, 1), half * CH:(half + 1) * CH, :]
                    dst = ring[:, slot, :].rearrange("p (k n) -> p k n", n=D)
                sp.dma_start(dst, src.rearrange("e (k p) n -> p (e k) n", p=P)).then_inc(full[slot], 16)

            for t in range(TT):
                sp.dma_start(acc[:, t, :], x_d[t]).then_inc(x_loaded[t], 16)
            for n in (C_Q, C_KV, C_U, C_GP):
                load_w_in(n, W_IN_LOAD.index(n))
            load_rows(W_POOL, w_pool_proj[0])
            load_w_in(C_GPA, W_IN_LOAD.index(C_GPA))
            load_rows(W_ATTN, w_attn_proj[0])
            sp.wait_ge(unit_done, UNIT["pool1"] + 1)
            sp.dma_start(bup, b_up_d).then_inc(bup_loaded, 16)
            sp.wait_ge(skew_written, 16)
            sp.dma_start(bdn, b_down[0]).then_inc(bdn_loaded, 16)
            sp.wait_ge(unit_done, UNIT["attn1"] + 1)
            load_w_in(C_GA, W_IN_LOAD.index(C_GA))
            load_w_in(C_GA2, W_IN_LOAD.index(C_GA2))
            load_rows(W_OUT0, w_out[0][0:CH, :])
            load_rows(W_OUT1, w_out[0][CH:D, :])
            last_use = ["gate_pool1", "u1", "gate_pool5", "gate_pool7", "gate_attn1", "gate_attn7",
                        "gate_attn5", "gate_attn7", "out3", "out3"]
            for load in range(LOADS):
                if load < R:
                    sp.wait_ge(unit_done, UNIT[last_use[load]] + 1)
                else:
                    sp.wait_ge(up_done, (load - R) // 2 + 1)
                load_expert((MIXER_LOADS + load) % R, load, 0)

            def wait_freed(g, load):
                back, g0 = load - R, 0
                if back < 0:
                    back, g0 = back + LOADS, -1
                if back < 2 * NJ:
                    sp.wait_ge(up_done, NJ * (g + g0) + back // 2 + 1)
                else:
                    sp.wait_ge(down_done, 2 * (g + g0) + (back - 2 * NJ) // 2 + 1)

            with sp.Fori(0, (PASSES - 1) // UNROLL) as i:
                for q in range(UNROLL):
                    g = i * UNROLL + (q + 1)
                    for load in range(LOADS):
                        wait_freed(g, load)
                        load_expert((MIXER_LOADS + (q + 1) * LOADS + load) % R, load, g * 2)

            sp.wait_ge(extra_ready, 1)
            extras = sp.value_load(n_extra[0:1, 0:1], min_val=0, max_val=LISTED)
            with sp.If(extras > 0):
                with sp.Fori(0, extras) as t:
                    pair = sp.value_load(x_pair[0:1, bass.ds(t, 1)], min_val=0, max_val=PASSES - 1)
                    for load in range(LOADS):
                        if load < R:
                            sp.wait_ge(down_done, (t + PASSES) * 2)
                        else:
                            sp.wait_ge(up_done, (t + PASSES) * NJ + ((load - R) // 2 + 1))
                        load_expert((ALL_LOADS + load - LOADS) % R, load, pair * 2)
            with sp.Else():
                pass
            sp.wait_ge(up_done, (extras + PASSES) * NJ - (NJ - 2))
            sp.dma_start(fin_g, final_g.partition_broadcast(P)).then_inc(fin_loaded, 16)
            for t in range(TT):
                sp.wait_ge(result_ready, t + 1)
                sp.dma_start(out_d[t], result[:, t, :]).then_inc(stored, 16)
            sp.wait_ge(stored, 16 * TT)

        @block.gpsimd
        def _(pool):
            nc.gpsimd.memset(rel[N_BUCKETS:N_BUCKETS + 1, :], 1.0).then_inc(consts, 1)
            pool.wait_ge(consts, 1)
            nc.gpsimd.memset(ident[:, :], 0.0).then_inc(consts, 1)
            nc.gpsimd.memset(eps, EPS).then_inc(consts, 1)
            pool.wait_ge(consts, 2)
            nc.gpsimd.affine_select(out=ident[:, :], in_=ident[:, :], compare_op=ALU.not_equal, fill=1.0,
                                    base=0, pattern=[[-1, P]], channel_multiplier=1).then_inc(consts, 1)
            nc.gpsimd.memset(uT[:, :, 0:PAD], 0.0).then_inc(consts, 1)
            for s in sums:
                nc.gpsimd.memset(s[:, :, 0:PAD], 0.0).then_inc(consts, 1)
            nc.gpsimd.memset(ones, 1.0).then_inc(consts, 1)
            nc.gpsimd.iota(ids_i, pattern=[[1, SLOTS]], base=0, channel_multiplier=0).then_inc(consts, 1)
            pool.wait_ge(consts, 8)
            nc.gpsimd.affine_select(out=before, in_=ones, compare_op=ALU.is_gt, fill=0.0,
                                    base=0, pattern=[[1, P]], channel_multiplier=-1).then_inc(consts, 1)
            pool.wait_ge(*emptied_at("bias_rows"))
            src = bias_row.unsqueeze(1).broadcast_to([HEADS, P, 3 * WINDOW])
            nc.gpsimd.dma_start(skew.rearrange("p h i -> h p i"), src).then_inc(skew_written, 16)
            pool.wait_ge(skew_written, 16)
            pitch = HEADS * 3 * WINDOW
            back = bass.AP(skew.tensor, WINDOW - 1, [[pitch - 1, P], [3 * WINDOW, HEADS], [1, 2 * WINDOW]])
            nc.gpsimd.dma_start(band, back).then_inc(band_loaded, 16)
            src = uT
            for step in range(NG):
                if step == 0:
                    pool.wait_ge(*emptied_at("u1"))
                else:
                    pool.wait_ge(summed, step)
                dst, far = sums[step % 2], 1 << step
                nc.gpsimd.tensor_tensor(dst[:, step:NG, PAD:], src[:, step:NG, PAD:],
                                        src[:, step:NG, PAD - far:PAD + SEQ - far], ALU.add).then_inc(summed, 1)
                src = dst

        @block.scalar
        def _(act):
            act.dma_start(rel[0:N_BUCKETS, :], rel_bias).then_inc(bias_in_loaded, 16)
            act.dma_start(bmap, buckets).then_inc(bias_in_loaded, 16)
            act.dma_start(vectors[0:KD, :], norm1_g[0].rearrange("(k p) -> k p", p=P)).then_inc(vec_loaded, 16)
            act.dma_start(vectors[KD:2 * KD, :], norm2_g[0].rearrange("(k p) -> k p", p=P)).then_inc(vec_loaded, 16)
            act.dma_start(vectors[2 * KD:2 * KD + KW, :], pool_scale[0].rearrange("(k p) -> k p", p=P)).then_inc(vec_loaded, 16)
            act.dma_start(pwt, pool_w[0].rearrange("g c d -> c g d")).then_inc(pw_loaded, 16)
            act.dma_start(snk, sinks[0].partition_broadcast(P)).then_inc(sinks_loaded, 16)
            act.dma_start(w_rt[:, :, :], w_router[0].rearrange("(k p) e -> p k e", p=P)).then_inc(router_loaded, 16)
            act.dma_start(b_rt[:, :], b_router[0].partition_broadcast(P)).then_inc(router_loaded, 16)

            steps = [0]

            def link(ins):
                steps[0] += 1
                ins.then_inc(act_step, 1)
                act.wait_ge(act_step, steps[0])

            def norm(t, dst, first):
                link(nc.scalar.activation(dst, acc[:, t, :], ACT.Square, accum_out=ss[:, t:t + 1]))
                nc.scalar.activation(std[:, t:t + 1], ss[:, t:t + 1], ACT.Sqrt, bias=eps,
                                     scale=1.0 / D).then_inc(std_ready, 1)
                act.wait_ge(rstd_ready, first + t + 1)
                nc.scalar.activation(dst, acc[:, t, :], ACT.Copy, scale=rstd[:, t:t + 1]).then_inc(xr_ready, 1)

            act.wait_ge(consts, 3)
            for t in range(TT):
                act.wait_ge(x_loaded[t], 16)
                norm(t, xr[:, t, :], 0)
            for i in range(2):
                act.wait_ge(unit_done, UNIT[f"q{i}"] + 1)
                nc.scalar.mul(qT[:, 2 * i:2 * i + 2, :].rearrange("p k t -> p (k t)"), bank[UNIT[f"q{i}"] % 8][:, :],
                              HD ** -0.5).then_inc(emptied["act"], 1)
            for i in range(2):
                act.wait_ge(unit_done, UNIT[f"pool{i}"] + 1)
                for g in (2 * i, 2 * i + 1):
                    ins = nc.scalar.activation(pooledT[:, g, :], bank[UNIT[f"pool{i}"] % 8][:, (g % 2) * SEQ:(g % 2 + 1) * SEQ],
                                               ACT.Copy, scale=psc[:, g:g + 1])
                ins.then_inc(emptied["act"], 1)
            act.wait_ge(negmax_ready, 1)
            for b, s in enumerate((scores0, scores1)):
                for h in range(HEADS):
                    nc.scalar.activation(s[:, h, :], s[:, h, :], ACT.Exp, bias=stat[:, 1, b, h:h + 1],
                                         accum_out=stat[:, 3, b, h:h + 1])
            nc.scalar.activation(stat[:, 2], stat[:, 2], ACT.Exp).then_inc(exp_ready, 1)
            gates = [f"gate_pool{c}" for c in range(KD)] + [f"gate_attn{c}" for c in range(KD)]

            def gate_sigmoid(n):
                u = UNIT[gates[n]]
                act.wait_ge(unit_done, u + 1)
                if n >= 2:
                    act.wait_ge(*emptied_at(gates[n - 2]))
                nc.scalar.activation(swi[:, (n % 2) * CF:(n % 2 + 1) * CF], bank[u % 8][:, 0:SEQ],
                                     ACT.Sigmoid).then_inc(sig_ready, 1)
            for c in range(KD):
                gate_sigmoid(c)
            for i in range(1, 6, 2):
                u = UNIT[f"probsT{i}"]
                act.wait_ge(unit_done, u + 1)
                dst = probsT1[:, 2 * i:2 * i + 2] if i < 4 else probsT0[:, 4 * (i - 4):4 * (i - 4) + 4]
                dst = dst.rearrange("p h k q -> p (h k q)") if i < 4 else dst.rearrange("p h q -> p (h q)")
                nc.scalar.copy(dst, bank[u % 8][:, :]).then_inc(emptied["act"], 1)
            for c in range(KD):
                gate_sigmoid(KD + c)
            link(nc.scalar.activation(warm, eps, ACT.Sqrt))
            for t in range(TT):
                act.wait_ge(*emptied_at(f"out{2 * t + 1}"))
                norm(t, x1r[:, t, :], TT)
            link(nc.scalar.activation(warm, eps, ACT.Exp))
            act.wait_ge(centred, 1)
            nc.scalar.activation(expd, dist_max, ACT.Exp).then_inc(expd_ready, 1)
            link(nc.scalar.activation(warm, eps, ACT.Sigmoid))
            act.wait_ge(unit_done, UNIT["gatesT"] + 1)
            nc.scalar.copy(gatesT, bank[UNIT["gatesT"] % 8][0:E, 0:SEQ]).then_inc(emptied["act"], 1)

            def copy_spreadT(g):
                act.wait_ge(spreadT_done, g + 1)
                nc.scalar.copy(spreadT, up_banks[0][:, 0:SEQ]).then_inc(spreadT_copied, 1)

            def copy_hidT(g, j):
                act.wait_ge(hidT_done, g * NJ + (j + 1))
                nc.scalar.copy(hidT[:, 2 * j:2 * j + 2, :].rearrange("p k s -> p (k s)"),
                               turn_banks[j % 2][:, 0:2 * P]).then_inc(hidT_copied, 1)

            def act_pass(g):
                for j in range(NJ):
                    act.wait_ge(glu_ready, g * NJ + (j + 1))
                    nc.scalar.activation(sig, glu, ACT.Sigmoid, scale=ALPHA).then_inc(sigmoid_ready, 1)
                    if j >= 1:
                        copy_hidT(g, j - 1)
                copy_hidT(g, NJ - 1)
                act.wait_ge(down_done, g * 2 + 2)
                nc.scalar.copy(y[:, 0:CH], down_banks[0][:, :]).then_inc(y0_copied, 1)

            copy_spreadT(0)
            with act.Fori(0, PASSES - 1) as g:
                act_pass(g)
                copy_spreadT(g + 1)
            act_pass(PASSES - 1)
            act.wait_ge(extra_ready, 1)
            extras = act.value_load(n_extra[0:1, 0:1], min_val=0, max_val=LISTED)
            with act.If(extras > 0):
                with act.Fori(0, extras) as t:
                    copy_spreadT(t + PASSES)
                    act_pass(t + PASSES)
            with act.Else():
                pass
            link(nc.scalar.activation(warm, eps, ACT.Sqrt))
            for t in range(TT):
                act.wait_ge(added, (extras + PASSES) * 4 + (2 * t + 2))
                steps[0] += 1
                nc.scalar.activation(result[:, t, :], acc[:, t, :], ACT.Square,
                                     accum_out=ss[:, t:t + 1]).then_inc(act_step, 1)
                act.wait_ge(act_step, steps[0])
                nc.scalar.activation(std[:, t:t + 1], ss[:, t:t + 1], ACT.Sqrt, bias=eps,
                                     scale=1.0 / D).then_inc(std_ready, 1)

        @block.tensor
        def _(pe):
            def begin(name):
                n = UNIT[name]
                if n >= 8:
                    pe.wait_ge(*emptied_at(UNITS[n - 8][0]))
                return bank[n % 8]

            pe.wait_ge(vec_loaded, 48)
            pe.wait_ge(consts, 4)
            b = begin("vectors")
            nc.tensor.transpose(b[:, 0:2 * KD + KW], vectors, ident[0:2 * KD + KW, 0:2 * KD + KW]).then_inc(unit_done, 1)
            pe.wait_ge(bias_in_loaded, 32)
            b = begin("bias_rows")
            nc.tensor.matmul(b[0:HEADS, 0:3 * WINDOW], rel, bmap, start=True, stop=True).then_inc(unit_done, 1)
            for m in range(4):
                b = begin(f"xT{m}")
                for k in (2 * m, 2 * m + 1):
                    for t in range(TT):
                        if m == 0 and k == 0:
                            pe.wait_ge(xr_ready, t + 1)
                        ins = nc.tensor.transpose(b[:, (k % 2) * SEQ + t * P:(k % 2) * SEQ + (t + 1) * P],
                                                  xr[:, t, k * P:(k + 1) * P], ident[:, :])
                ins.then_inc(unit_done, 1)

            def chunk(n, wide=CH):
                return ring[:, n % R, 0:KD * wide].rearrange("p (k n) -> p k n", k=KD)

            def project(dst, w, c, rhs, kn):
                for k in range(kn):
                    ins = nc.tensor.matmul(dst, w[:, k, c * P:(c + 1) * P], rhs[:, k, :], start=(k == 0), stop=(k == kn - 1))
                return ins

            pe.wait_ge(*load_at(C_Q))
            pe.wait_ge(*emptied_at("xT3"))
            for i in range(2):
                b = begin(f"q{i}")
                for c in (2 * i, 2 * i + 1):
                    ins = project(b[:, (c % 2) * SEQ:(c % 2 + 1) * SEQ], chunk(C_Q), c, hT, KD)
                ins.then_inc(unit_done, 1)
            pe.wait_ge(*load_at(C_KV))
            b = begin("kv")
            project(b[:, 0:SEQ], chunk(C_KV), 0, hT, KD)
            for t in range(TT):
                for k in range(KD):
                    ins = nc.tensor.matmul(b[:, SEQ + t * P:SEQ + (t + 1) * P], hT[:, k, t * P:(t + 1) * P],
                                           chunk(C_KV)[:, k, P:2 * P], start=(k == 0), stop=(k == KD - 1))
            ins.then_inc(unit_done, 1)
            pe.wait_ge(*load_at(C_U))
            for i in range(2):
                b = begin(f"u{i}")
                for c in (2 * i, 2 * i + 1):
                    ins = project(b[:, (c % 2) * SEQ:(c % 2 + 1) * SEQ], chunk(C_U), c, hT, KD)
                ins.then_inc(unit_done, 1)
            pe.wait_ge(*emptied_at("q1"))
            pe.wait_ge(*emptied_at("kv"))
            for blk, keys, groups in ((1, 2 * WINDOW, ((0, 1, 2, 3), (4, 5, 6, 7))), (0, WINDOW, (tuple(range(8)),))):
                for n, hs in enumerate(groups):
                    bs = [begin(f"scores{blk}_{2 * n + odd}") for odd in range(2)]
                    for at, h in enumerate(hs):
                        lo = HD * (h % 2)
                        ins = nc.tensor.matmul(bs[h % 2][:, (at // 2) * keys:(at // 2 + 1) * keys],
                                               qT[lo:lo + HD, h // 2, blk * P:(blk + 1) * P],
                                               kT[lo:lo + HD, h // 4, 0:keys], start=True, stop=True)
                        if at >= len(hs) - 2:
                            ins.then_inc(unit_done, 1)
            pe.wait_ge(pw_loaded, 16)
            pe.wait_ge(z_ready, 1)
            for i in range(2):
                b = begin(f"pool{i}")
                for g in (2 * i, 2 * i + 1):
                    ins = nc.tensor.matmul(b[:, (g % 2) * SEQ:(g % 2 + 1) * SEQ], pwt[:, g, :], zT[:, g, :], start=True, stop=True)
                ins.then_inc(unit_done, 1)

            def gated(kind, at, w_load, rhs):
                for c in range(KD):
                    n = W_IN_LOAD[(at + c * P) // CH]
                    pe.wait_ge(*load_at(n))
                    wide = CH if n != C_GA2 else CH // 2
                    b = begin(f"{kind}{c}")
                    project(b[:, 0:SEQ], chunk(n, wide), (at + c * P) % CH // P, hT, KD)
                    if c == 0:
                        pe.wait_ge(*load_at(w_load))
                    w = ring[:, w_load % R, :].rearrange("p (k n) -> p k n", n=D)
                    project(b[:, SEQ:2 * SEQ], w, c, rhs, KW).then_inc(unit_done, 1)

            pe.wait_ge(*emptied_at("pool1"))
            gated("gate_pool", GATE_POOL_AT, W_POOL, pooledT)
            for i in range(6):
                b = begin(f"probsT{i}")
                if i == 0:
                    pe.wait_ge(probs_ready, 1)
                for n in range(4):
                    if i < 4:
                        src = scores1[:, 2 * i + n // 2, (n % 2) * P:(n % 2 + 1) * P]
                    else:
                        src = scores0[:, 4 * (i - 4) + n, :]
                    ins = nc.tensor.transpose(b[:, n * P:(n + 1) * P], src, ident[:, :])
                ins.then_inc(unit_done, 1)
            for i in range(2):
                b = begin(f"attn{i}")
                if i == 0:
                    pe.wait_ge(*emptied_at("probsT4"))
                    pe.wait_ge(*emptied_at("probsT5"))
                for hp in (2 * i, 2 * i + 1):
                    at = (hp % 2) * SEQ
                    for blk, kt in ((0, 0), (1, 0), (1, 1)):
                        for h in (2 * hp, 2 * hp + 1):
                            lo = HD * (h % 2)
                            rhs = probsT1[:, h, kt, :] if blk else probsT0[:, h, :]
                            ins = nc.tensor.matmul(b[lo:lo + HD, at + blk * P:at + (blk + 1) * P],
                                                   vv[:, kt, HD * (h // 4):HD * (h // 4 + 1)], rhs,
                                                   start=(kt == 0), stop=(blk == kt))
                ins.then_inc(unit_done, 1)
            pe.wait_ge(*emptied_at("attn1"))
            gated("gate_attn", GATE_ATTN_AT, W_ATTN, attnT)
            pe.wait_ge(*load_at(W_OUT0))
            pe.wait_ge(*load_at(W_OUT1))
            pe.wait_ge(mixed_ready, KD)
            for q in range(4):
                t, n = q // 2, q % 2
                b = begin(f"out{q}")
                for k in range(KD):
                    w = ring[:, (W_OUT0 + k // 4) % R, :].rearrange("p (k n) -> p k n", n=D)
                    ins = nc.tensor.matmul(b[:, :], mixedT[:, k, t * P:(t + 1) * P], w[:, k % 4, n * CH:(n + 1) * CH],
                                           start=(k == 0), stop=(k == KD - 1))
                ins.then_inc(unit_done, 1)
            for t in range(TT):
                pe.wait_ge(xr_ready, TT + t + 1)
                for half in range(2):
                    b = begin(f"h2T{2 * t + half}")
                    for k in range(4):
                        ins = nc.tensor.transpose(b[:, k * P:(k + 1) * P],
                                                  x1r[:, t, (4 * half + k) * P:(4 * half + k + 1) * P], ident[:, :])
                    ins.then_inc(unit_done, 1)
            pe.wait_ge(router_loaded, 32)
            for t in range(TT):
                b = begin(f"logits{t}")
                pe.wait_ge(*emptied_at(f"h2T{2 * t + 1}"))
                for k in range(KD):
                    ins = nc.tensor.matmul(b[:, 0:E], h2T[t][:, k, :], w_rt[:, k, :], start=(k == 0), stop=(k == KD - 1))
                ins.then_inc(unit_done, 1)
            pe.wait_ge(consts, 10)
            pe.wait_ge(chosen_ready, 1)
            b = begin("ranks")
            nc.tensor.matmul(b[:, 0:E], before, chosen[:, 0, :], start=True, stop=True)
            nc.tensor.matmul(b[:, E:2 * E], before, chosen[:, 1, :], start=True, stop=False)
            nc.tensor.matmul(b[:, E:2 * E], ones, chosen[:, 0, :], start=False, stop=True)
            nc.tensor.matmul(b[:, 2 * E:3 * E], ones, chosen[:, 0, :], start=True, stop=False)
            nc.tensor.matmul(b[:, 2 * E:3 * E], ones, chosen[:, 1, :], start=False, stop=True).then_inc(unit_done, 1)
            pe.wait_ge(gates_ready, 1)
            b = begin("gatesT")
            for t in range(TT):
                ins = nc.tensor.transpose(b[0:E, t * P:(t + 1) * P], gate[:, t, :], ident[:, :])
            ins.then_inc(unit_done, 1)

            def gather(g):
                pe.wait_ge(spread_ready, g + 1)
                for k in range(KD):
                    for t in range(TT):
                        ins = nc.tensor.matmul(turn_banks[k // 4][:, (k % 4) * P:(k % 4 + 1) * P], x1r[:, t, k * P:(k + 1) * P],
                                               pick[:, t, :], start=(t == 0), stop=(t == TT - 1))
                    if k % 4 == 3:
                        ins.then_inc(gather_done, 1)

            def turn_spread():
                for t in range(TT):
                    ins = nc.tensor.transpose(up_banks[0][:, t * P:(t + 1) * P], spread[:, t, :], ident[:, :])
                ins.then_inc(spreadT_done, 1)

            def turn_hid(g, j):
                pe.wait_ge(hid_ready, g * NJ + (j + 1))
                if j >= 2:
                    pe.wait_ge(hidT_copied, g * NJ + (j - 1))
                for c in range(2):
                    ins = nc.tensor.transpose(turn_banks[j % 2][:, c * P:(c + 1) * P],
                                              hid[:, (2 * j + c) * P:(2 * j + c + 1) * P], ident[:, :])
                ins.then_inc(hidT_done, 1)

            def pe_pass(g, slot_load, following):
                for j in range(NJ):
                    b = up_banks[j % 2]
                    if j == 0:
                        pe.wait_ge(spreadT_copied, g + 1)
                        pe.wait_ge(rows_ready, g + 1)
                    nc.tensor.matmul(b[:, :], rows[:, j].rearrange("p e s -> p (e s)"), bup, start=True, stop=False,
                                     skip_group_check=True)
                    if j == 0:
                        pe.wait_ge(xg_copied, g * 2 + 2)
                    w = [slot_load(2 * j + e).rearrange("p (k n) -> p k n", n=CH) for e in range(2)]
                    for k in range(KD):
                        for e in range(2):
                            ins = nc.tensor.matmul(b[e * SLOTS:(e + 1) * SLOTS, :], xgT[:, k, e * SLOTS:(e + 1) * SLOTS],
                                                   w[e][:, k, :], start=False, stop=(k == KD - 1), skip_group_check=True)
                    ins.then_inc(up_done, 1)
                    if j >= 1:
                        turn_hid(g, j - 1)
                for half in range(2):
                    w = [slot_load(2 * NJ + 2 * half + e).rearrange("p (k n) -> p k n", n=D) for e in range(2)]
                    for k in range(4 * half, 4 * half + 4):
                        if k % 2 == 0:
                            pe.wait_ge(hidT_copied, g * NJ + (k // 2 + 1))
                        for n in range(2):
                            for e in range(2):
                                ins = nc.tensor.matmul(down_banks[n][e * SLOTS:(e + 1) * SLOTS, :],
                                                       hidT[:, k, e * SLOTS:(e + 1) * SLOTS],
                                                       w[e][:, k % 4, n * CH:(n + 1) * CH],
                                                       start=(k == 0), stop=(k == KD - 1), skip_group_check=True)
                    ins.then_inc(down_done, 1)
                    if half == 0:
                        turn_hid(g, NJ - 1)
                if following:
                    gather(g + 1)
                pe.wait_ge(y0_copied, g + 1)
                pe.wait_ge(y1_copied, g + 1)
                for q in range(4):
                    t, n = q // 2, q % 2
                    pe.wait_ge(added, g * 4 + (q + 3))
                    nc.tensor.matmul(scatter_banks[q % 2][:, :], spreadT[:, t * P:(t + 1) * P], y[:, n * CH:(n + 1) * CH],
                                     start=True, stop=True).then_inc(scatter_done, 1)
                if following:
                    turn_spread()

            pe.wait_ge(*emptied_at("gatesT"))
            gather(0)
            turn_spread()
            pe.wait_ge(bdn_loaded, 16)
            for q in range(4):
                t, n = q // 2, q % 2
                if q >= 2:
                    pe.wait_ge(added, q - 1)
                nc.tensor.matmul(scatter_banks[q % 2][:, :], gatesT[:, t * P:(t + 1) * P], bdn[:, n * CH:(n + 1) * CH],
                                 start=True, stop=True).then_inc(scatter_done, 1)
            pe.wait_ge(bup_loaded, 16)
            pe.wait_ge(added, 4)

            def main_slot(i, q):
                def slot_load(load):
                    n = MIXER_LOADS + q * LOADS + load
                    pe.wait_ge(full[n % R], i * (16 * UNROLL * LOADS // R) + 16 * (n // R + 1))
                    return ring[:, n % R, :]
                return slot_load

            with pe.Fori(0, (PASSES - 1) // UNROLL) as i:
                for q in range(UNROLL):
                    pe_pass(i * UNROLL + q, main_slot(i, q), True)
            pe_pass(PASSES - 1, main_slot((PASSES - 1) // UNROLL, 0), False)

            pe.wait_ge(extra_ready, 1)
            extras = pe.value_load(n_extra[0:1, 0:1], min_val=0, max_val=LISTED)
            extra_slots = [(ALL_LOADS + load - LOADS) % R for load in range(LOADS)]
            with pe.If(extras > 0):
                with pe.Fori(0, extras) as t:
                    def slot_load(load):
                        slot = extra_slots[load]
                        landed = len(range(slot, ALL_LOADS, R))
                        pe.wait_ge(full[slot], t * (16 * extra_slots.count(slot))
                                   + 16 * (landed + extra_slots[:load + 1].count(slot)))
                        return ring[:, slot, :]
                    gather(t + PASSES)
                    turn_spread()
                    pe_pass(t + PASSES, slot_load, False)
            with pe.Else():
                pass

        @block.vector
        def _(dve):
            steps = [0]

            def link(ins):
                steps[0] += 1
                ins.then_inc(dve_step, 1)
                dve.wait_ge(dve_step, steps[0])

            def unit(name):
                dve.wait_ge(unit_done, UNIT[name] + 1)
                return bank[UNIT[name] % 8]

            def empties(ins):
                ins.then_inc(emptied["dve"], 1)

            def invert_std(t, first):
                dve.wait_ge(std_ready, first + t + 1)
                nc.vector.reciprocal(rstd[:, t:t + 1], std[:, t:t + 1]).then_inc(rstd_ready, 1)

            b = unit("vectors")
            empties(nc.vector.tensor_copy(vecT, b[:, 0:2 * KD + KW]))
            b = unit("bias_rows")
            empties(nc.vector.tensor_copy(bias_row, b[0:HEADS, 0:3 * WINDOW]))
            dve.wait_ge(consts, 9)
            link(nc.vector.tensor_copy(ids0[:, :], ids_i))
            for g, w in enumerate(POOL_WINDOWS):
                ins = nc.vector.tensor_scalar(inv_cnt[:, g, :], ids0[:, 0:PAD], 1.0, float(w), ALU.add, ALU.min)
            link(ins)
            link(nc.vector.reciprocal(inv_cnt[:, :, :], inv_cnt[:, :, :]))
            link(nc.vector.tensor_scalar(ids0[:, :], ids0[:, :], -UNRANKED, None, ALU.add))
            link(nc.vector.tensor_copy(ids[:, :], ids0[:, :]))
            for t in range(TT):
                invert_std(t, 0)
            dve.wait_ge(*emptied_at("vectors"))
            for m in range(4):
                b = unit(f"xT{m}")
                empties(nc.vector.tensor_tensor(hT[:, 2 * m:2 * m + 2, :], b[:, :].rearrange("p (k t) -> p k t", k=2),
                                                g1[:, 2 * m:2 * m + 2].unsqueeze(2).broadcast_to([P, 2, SEQ]), ALU.mult))
            b = unit("kv")
            for kv in range(KV_HEADS):
                for half in range(2):
                    nc.vector.tensor_copy(kT[half * HD:(half + 1) * HD, kv, :], b[kv * HD:(kv + 1) * HD, 0:SEQ])
            empties(nc.vector.tensor_copy(vv.rearrange("p t d -> p (t d)"), b[:, SEQ:2 * SEQ]))
            dve.wait_ge(consts, 7)
            for i in range(2):
                b = unit(f"u{i}")
                empties(nc.vector.tensor_copy(uT[:, 2 * i:2 * i + 2, PAD:], b[:, :].rearrange("p (g t) -> p g t", g=2)))
            dve.wait_ge(band_loaded, 16)
            for n in range(4):
                b = unit(f"scores1_{n}")
                h0 = 4 * (n // 2) + n % 2
                empties(nc.vector.tensor_tensor(scores1[:, h0:h0 + 3:2, :], b[:, :].rearrange("p (h k) -> p h k", h=2),
                                                band[:, h0:h0 + 3:2, :], ALU.add))
            for n in range(2):
                b = unit(f"scores0_{n}")
                empties(nc.vector.tensor_tensor(scores0[:, n:HEADS:2, :], b[:, :].rearrange("p (h k) -> p h k", h=4),
                                                band[:, n:HEADS:2, WINDOW:], ALU.add))
            dve.wait_ge(summed, NG)
            dve.wait_ge(*emptied_at("u1"))
            for g, w in enumerate(POOL_WINDOWS):
                nc.vector.scalar_tensor_tensor(zT[:, g, :], sums[g % 2][:, g, PAD:], 1.0 / w, uT[:, g, PAD:], ALU.mult, ALU.subtract)
                ins = nc.vector.tensor_tensor(head[:, g, :], sums[g % 2][:, g, PAD:2 * PAD], inv_cnt[:, g, :], ALU.mult)
            link(ins)
            nc.vector.tensor_tensor(zT[:, :, 0:PAD], head[:, :, :], uT[:, :, PAD:2 * PAD], ALU.subtract).then_inc(z_ready, 1)
            dve.wait_ge(sinks_loaded, 16)
            dve.wait_ge(*emptied_at("scores0_1"))
            nc.vector.tensor_reduce(stat[:, 0, 0, :], scores0, AX.X, ALU.max)
            link(nc.vector.tensor_reduce(stat[:, 0, 1, :], scores1, AX.X, ALU.max))
            sink2 = snk.unsqueeze(1).broadcast_to([P, 2, HEADS])
            link(nc.vector.tensor_tensor(stat[:, 0], stat[:, 0], sink2, ALU.max))
            nc.vector.tensor_tensor(stat[:, 2], sink2, stat[:, 0], ALU.subtract)
            nc.vector.tensor_scalar(stat[:, 1], stat[:, 0], -1.0, None, ALU.mult).then_inc(negmax_ready, 1)
            dve.wait_ge(exp_ready, 1)
            link(nc.vector.tensor_tensor(stat[:, 3], stat[:, 3], stat[:, 2], ALU.add))
            link(nc.vector.reciprocal(stat[:, 4], stat[:, 3]))
            nc.vector.tensor_tensor(scores0, scores0, stat[:, 4, 0, :].unsqueeze(2).broadcast_to([P, HEADS, WINDOW]), ALU.mult)
            nc.vector.tensor_tensor(scores1, scores1, stat[:, 4, 1, :].unsqueeze(2).broadcast_to([P, HEADS, 2 * WINDOW]),
                                    ALU.mult).then_inc(probs_ready, 1)

            def gated(kind, c, n):
                b = unit(f"{kind}{c}")
                dve.wait_ge(sig_ready, n + 1)
                s = swi[:, (n % 2) * CF:(n % 2 + 1) * CF]
                if kind == "gate_pool":
                    empties(nc.vector.tensor_tensor(mixedT[:, c, :], s, b[:, SEQ:2 * SEQ], ALU.mult))
                else:
                    if c >= 1:
                        dve.wait_ge(mixed_ready, c)
                    empties(nc.vector.tensor_tensor(swi[:, 2 * CF:3 * CF], s, b[:, SEQ:2 * SEQ], ALU.mult))
                    dve.wait_ge(*emptied_at(f"{kind}{c}"))
                    nc.vector.tensor_tensor(mixedT[:, c, :], mixedT[:, c, :], swi[:, 2 * CF:3 * CF], ALU.add).then_inc(mixed_ready, 1)

            for c in range(KD):
                gated("gate_pool", c, c)
            for i in range(0, 6, 2):
                b = unit(f"probsT{i}")
                dst = probsT1[:, 2 * i:2 * i + 2] if i < 4 else probsT0[:, 4 * (i - 4):4 * (i - 4) + 4]
                dst = dst.rearrange("p h k q -> p (h k q)") if i < 4 else dst.rearrange("p h q -> p (h q)")
                empties(nc.vector.tensor_copy(dst, b[:, :]))
            for i in range(2):
                b = unit(f"attn{i}")
                empties(nc.vector.tensor_copy(attnT[:, 2 * i:2 * i + 2, :].rearrange("p k t -> p (k t)"), b[:, :]))
            for c in range(KD):
                gated("gate_attn", c, KD + c)
            for t in range(TT):
                for n in range(2):
                    b = unit(f"out{2 * t + n}")
                    empties(nc.vector.tensor_tensor(acc[:, t, n * CH:(n + 1) * CH], acc[:, t, n * CH:(n + 1) * CH], b[:, :], ALU.add))
                if t == 0:
                    invert_std(0, TT)
            invert_std(1, TT)
            for t in range(TT):
                for half in range(2):
                    b = unit(f"h2T{2 * t + half}")
                    empties(nc.vector.tensor_tensor(h2T[t][:, 4 * half:4 * half + 4, :], b[:, :].rearrange("p (k t) -> p k t", k=4),
                                                    g2[:, 4 * half:4 * half + 4].unsqueeze(2).broadcast_to([P, 4, P]), ALU.mult))
            dve.wait_ge(router_loaded, 32)
            for t in range(TT):
                b = unit(f"logits{t}")
                empties(nc.vector.tensor_tensor(logits[:, t, :], b[:, 0:E], b_rt[:, :], ALU.add))
                dve.wait_ge(*emptied_at(f"logits{t}"))
                ins = nc.vector.max(top[:, t, :], logits[:, t, :])
            link(ins)
            fourth = top[:, :, TOP_K - 1:TOP_K].broadcast_to([P, TT, E])
            nc.vector.tensor_tensor(dist_max, logits, top[:, :, 0:1].broadcast_to([P, TT, E]), ALU.subtract).then_inc(centred, 1)
            nc.vector.tensor_tensor(above, logits, fourth, ALU.is_gt)
            link(nc.vector.tensor_tensor(equal, logits, fourth, ALU.is_equal))
            nc.vector.tensor_reduce(most, above, AX.X, ALU.add)
            dve.wait_ge(consts, 9)
            for t in range(TT):
                ins = nc.vector.tensor_tensor_scan(count_eq[:, t, :], ones[:, 0:E], equal[:, t, :], 0.0, ALU.mult, ALU.add)
            link(ins)
            link(nc.vector.tensor_scalar(more, most, -1.0, float(TOP_K), ALU.mult, ALU.add))
            link(nc.vector.tensor_tensor(count_eq, count_eq, more.unsqueeze(2).broadcast_to([P, TT, E]), ALU.is_le))
            link(nc.vector.tensor_tensor(equal, equal, count_eq, ALU.mult))
            nc.vector.tensor_tensor(chosen, above, equal, ALU.add).then_inc(chosen_ready, 1)
            dve.wait_ge(chosen_ready, 1)
            dve.wait_ge(expd_ready, 1)
            link(nc.vector.tensor_tensor(expd, expd, chosen, ALU.mult))
            link(nc.vector.tensor_reduce(gsum, expd, AX.X, ALU.add))
            link(nc.vector.reciprocal(ginv, gsum))
            nc.vector.tensor_tensor(gate[:, :, :], expd, ginv.unsqueeze(2).broadcast_to([P, TT, E]), ALU.mult).then_inc(gates_ready, 1)
            b = unit("ranks")
            nc.vector.tensor_copy(served[:, :], b[:, 2 * E:3 * E])
            empties(nc.vector.scalar_tensor_tensor(rank[:, :, :].rearrange("p t e -> p (t e)"), chosen.rearrange("p t e -> p (t e)"),
                                                   -UNRANKED, b[:, 0:2 * E], ALU.mult, ALU.add))
            dve.wait_ge(*emptied_at("ranks"))
            dve.wait_ge(gates_ready, 1)

            def build(g, pair):
                ids4 = ids[:, :].unsqueeze(1).unsqueeze(1).broadcast_to([P, TT, 2, SLOTS])
                pick4 = pick.rearrange("p t (e s) -> p t e s", e=2)
                spread4 = spread.rearrange("p t (e s) -> p t e s", e=2)
                two = bass.ds(pair * 2, 2)
                nc.vector.tensor_tensor(pick4, ids4, rank[:, :, two].unsqueeze(3).broadcast_to([P, TT, 2, SLOTS]),
                                        ALU.is_equal).then_inc(pick_ready, 1)
                for e in range(2):
                    ins = nc.vector.tensor_copy(
                        rows[:, :, e, :], ident[:, bass.ds(pair * 8 + 4 * e, NJ)].unsqueeze(2).broadcast_to([P, NJ, SLOTS]))
                ins.then_inc(rows_ready, 1)
                dve.wait_ge(pick_ready, g + 1)
                nc.vector.tensor_tensor(spread4, pick4, gate[:, :, two].unsqueeze(3).broadcast_to([P, TT, 2, SLOTS]),
                                        ALU.mult).then_inc(spread_ready, 1)

            def copy_xg(g):
                for n in range(2):
                    dve.wait_ge(gather_done, g * 2 + (n + 1))
                    nc.vector.tensor_tensor(xgT[:, 4 * n:4 * n + 4, :], turn_banks[n][:, :].rearrange("p (k s) -> p k s", k=4),
                                            g2[:, 4 * n:4 * n + 4].unsqueeze(2).broadcast_to([P, 4, P]), ALU.mult).then_inc(xg_copied, 1)

            def add(q):
                t, n = q // 2, q % 2
                nc.vector.tensor_tensor(acc[:, t, n * CH:(n + 1) * CH], acc[:, t, n * CH:(n + 1) * CH],
                                        scatter_banks[q % 2][:, :], ALU.add).then_inc(added, 1)

            def dve_pass(g, following):
                for j in range(NJ):
                    dve.wait_ge(up_done, g * NJ + (j + 1))
                    if j >= 1:
                        dve.wait_ge(hid_ready, g * NJ + j)
                    pairs = up_banks[j % 2][:, :].rearrange("p (f two) -> p f two", two=2)
                    nc.vector.tensor_scalar(glu, pairs[:, :, 0], LIMIT, None, ALU.min).then_inc(glu_ready, 1)
                    nc.vector.tensor_scalar(lin, pairs[:, :, 1], -LIMIT, LIMIT, ALU.max, ALU.min).then_inc(lin_ready, 1)
                    dve.wait_ge(lin_ready, g * NJ + (j + 1))
                    nc.vector.scalar_tensor_tensor(lin, lin, 1.0, glu, ALU.add, ALU.mult).then_inc(gated_ready, 1)
                    dve.wait_ge(gated_ready, g * NJ + (j + 1))
                    dve.wait_ge(sigmoid_ready, g * NJ + (j + 1))
                    nc.vector.tensor_tensor(hid[:, j * CF:(j + 1) * CF], lin, sig, ALU.mult).then_inc(hid_ready, 1)
                if following:
                    build(g + 1, g + 1)
                dve.wait_ge(down_done, g * 2 + 2)
                nc.vector.tensor_copy(y[:, CH:2 * CH], down_banks[1][:, :]).then_inc(y1_copied, 1)
                if following:
                    copy_xg(g + 1)
                for q in range(4):
                    dve.wait_ge(scatter_done, g * 4 + (q + 5))
                    add(q)

            build(0, 0)
            copy_xg(0)
            for q in range(4):
                dve.wait_ge(scatter_done, q + 1)
                add(q)
            n_codes = ROUNDS * PASSES
            code, want, left = extra[:, 0:n_codes], extra[:, 48:48 + n_codes], extra[:, 96:96 + n_codes]
            fuller, best, live = extra[:, 144:160], extra[:, 160:176], extra[:, 176:192]
            count, code_i, round_i = extra[:, 192:193], extra[:, 208:224].bitcast(I32), extra[:, 224:240].bitcast(I32)
            nc.vector.tensor_scalar(code, ids0[:, 0:n_codes], -1.0, n_codes - UNRANKED, ALU.mult, ALU.add)
            both = served[:, :].rearrange("p (g e) -> p g e", e=2)
            link(nc.vector.tensor_tensor(fuller, both[:, :, 0], both[:, :, 1], ALU.max))
            for r in range(ROUNDS):
                part = slice(r * PASSES, (r + 1) * PASSES)
                ins = nc.vector.scalar_tensor_tensor(want[:, part], fuller, float(SLOTS * (r + 1)), code[:, part], ALU.is_gt, ALU.mult)
            link(ins)
            link(nc.vector.max(best[:, 0:8], want))
            link(nc.vector.match_replace(left, best[:, 0:8], want, 0.0))
            link(nc.vector.max(best[:, 8:16], left))
            nc.vector.tensor_scalar(code_i, best, -1.0, float(n_codes), ALU.mult, ALU.add)
            link(nc.vector.tensor_scalar(live, best, 0.5, None, ALU.is_gt))
            link(nc.vector.tensor_reduce(count, live, AX.X, ALU.add))
            nc.vector.tensor_scalar(x_pair[:, :], code_i, PASSES - 1, None, ALU.bitwise_and)
            link(nc.vector.tensor_scalar(round_i, code_i, PASSES.bit_length() - 1, None, ALU.logical_shift_right))
            nc.vector.tensor_scalar(x_off[:, :], round_i, float(SLOTS), float(SLOTS), ALU.mult, ALU.add)
            nc.vector.tensor_copy(n_extra[:, :], count).then_inc(extra_ready, 1)
            dve.wait_ge(extra_ready, 1)
            extras = dve.value_load(n_extra[0:1, 0:1], min_val=0, max_val=LISTED)

            with dve.Fori(0, PASSES - 1) as g:
                dve_pass(g, True)
            dve_pass(PASSES - 1, False)
            with dve.If(extras > 0):
                with dve.Fori(0, extras) as t:
                    pair = dve.value_load(x_pair[0:1, bass.ds(t, 1)], min_val=0, max_val=PASSES - 1)
                    nc.vector.tensor_scalar(ids[:, :], ids0[:, :], x_off[:, bass.ds(t, 1)], None, ALU.add).then_inc(ids_ready, 1)
                    dve.wait_ge(ids_ready, t + 1)
                    build(t + PASSES, pair)
                    copy_xg(t + PASSES)
                    dve_pass(t + PASSES, False)
            with dve.Else():
                pass
            for t in range(TT):
                invert_std(t, 2 * TT)
                dve.wait_ge(rstd_ready, 2 * TT + t + 1)
                if t == 0:
                    dve.wait_ge(fin_loaded, 16)
                nc.vector.scalar_tensor_tensor(result[:, t, :], acc[:, t, :], rstd[:, t:t + 1], fin_g, ALU.mult,
                                               ALU.mult).then_inc(result_ready, 1)


_INS = ["x", "norm1_g", "w_in", "pool_w", "pool_scale", "w_pool_proj", "sinks", "w_attn_proj", "w_out", "norm2_g",
        "w_router", "b_router", "w_up", "b_up", "w_down", "b_down", "rel_bias", "final_g"]


def kernel(**inputs):
    import concourse.bacc as bacc
    from concourse.bass_utils import run_bass_kernel_spmd

    nc = bacc.Bacc("TRN2", target_bir_lowering=False, num_devices=1)
    arrays, args = {}, []
    for name in _INS:
        a = np.ascontiguousarray(inputs[name])
        arrays[f"in_{name}"] = a
        args.append(nc.dram_tensor(f"in_{name}", a.shape, mybir.dt.from_np(a.dtype), kind="ExternalInput").ap())
    arrays["in_buckets"] = bucket_map()
    args.append(nc.dram_tensor("in_buckets", arrays["in_buckets"].shape, F32, kind="ExternalInput").ap())
    out = nc.dram_tensor("out", (1, SEQ, D), F32, kind="ExternalOutput").ap()
    hybrid_block_kernel(nc, *args, out)
    r = run_bass_kernel_spmd(nc, [arrays], core_ids=[0])
    return r.results[0]["out"]
```

```python
import math
from contextlib import ExitStack

import numpy as np

import concourse.bass as bass
from concourse import mybir

F32 = mybir.dt.float32
I32 = mybir.dt.int32
ALU = mybir.AluOpType
ACT = mybir.ActivationFunctionType
AX = mybir.AxisListType

P = 128
D = 1024
SEQ = 256
TT = SEQ // P
KD = D // P
POOL_WIDTH = 512
POOL_WINDOWS = (2, 4, 8, 16)
NG = len(POOL_WINDOWS)
PAD = max(POOL_WINDOWS)
HEADS, KV_HEADS, HD = 8, 2, 64
ATTN_WIDTH = HEADS * HD
KW = ATTN_WIDTH // P
WINDOW = 128
N_BUCKETS, MAX_DISTANCE = 32, 128
MASKED = -1e30
E, TOP_K = 32, 4
LIMIT, ALPHA, EPS = 7.0, 1.702, 1e-5

SLOTS = P // 2
PASSES = E // 2
ROUNDS = SEQ // SLOTS - 1
LISTED = 16
NJ, CH = 4, 512
CF = CH // 2
UNRANKED = 1024.0

R = 10
SLOT = KD * CH
LANDED = 32
C_U, C_KV, C_Q, C_GP, W_POOL, C_GPA, W_ATTN, C_GA, C_GA2, W_OUT0, W_OUT1 = range(11)
MIXER_LOADS = 11
W_IN_LOAD = [C_U, C_Q, C_KV, C_GP, C_GPA, C_GA, C_GA2]
GATE_POOL_AT = POOL_WIDTH + ATTN_WIDTH + 2 * KV_HEADS * HD
GATE_ATTN_AT = GATE_POOL_AT + D
LOADS = 12
UP_LOADS = 2 * NJ
UNROLL = 5
ALL_LOADS = MIXER_LOADS + PASSES * LOADS

UNITS = ([("vectors", "dve"), ("bias_rows", "dve")]
         + [(f"xT{m}", "dve") for m in range(4)]
         + [("u0", "dve"), ("u1", "dve"), ("kv", "dve"), ("q0", "act"), ("q1", "act")]
         + [("pool0", "act"), ("pool1", "act")]
         + [(f"scores1_{i}", "dve") for i in range(4)] + [(f"scores0_{i}", "dve") for i in range(2)]
         + [(f"gate_pool{c}", "dve") for c in range(KD - 1)]
         + [(f"probsT{i}", "act" if i % 2 else "dve") for i in range(6)]
         + [(f"gate_pool{KD - 1}", "dve"), ("attn0", "dve"), ("attn1", "dve")]
         + [(f"gate_attn{c}", "dve") for c in range(KD)]
         + [("out0", "dve"), ("out1", "dve"), ("out2", "dve"), ("x1T0", "dve"), ("x1T1", "dve"), ("logits0", "dve")]
         + [("x1T2", "dve"), ("out3", "dve"), ("x1T3", "dve"), ("logits1", "dve"), ("ranks", "dve"), ("served", "dve")])
UNIT = {name: n for n, (name, _) in enumerate(UNITS)}


def t5_bucket(dist):
    max_exact = N_BUCKETS // 2
    d = np.maximum(dist, 1).astype(np.float32)
    large = max_exact + (np.log(d / max_exact) / math.log(MAX_DISTANCE / max_exact)
                         * (N_BUCKETS - max_exact)).astype(np.int32)
    large = np.minimum(large, N_BUCKETS - 1)
    return np.where(dist < max_exact, dist, large).astype(np.int32)


def bucket_map():
    dist = 2 * WINDOW - 1 - np.arange(3 * WINDOW)
    inside = (dist >= 0) & (dist < WINDOW)
    rows = np.zeros((N_BUCKETS + 1, 3 * WINDOW), np.float32)
    rows[t5_bucket(np.clip(dist, 0, None))[inside], np.flatnonzero(inside)] = 1.0
    rows[N_BUCKETS, ~inside] = MASKED
    return rows


def hybrid_block_kernel(nc, x, norm1_g, w_in, pool_w, pool_scale, w_pool_proj, sinks, w_attn_proj,
                        w_out, norm2_g, w_router, b_router, w_up, b_up, w_down, b_down, rel_bias,
                        final_g, buckets, out):
    x_d = x.rearrange("b (t p) d -> (b t) p d", p=P)
    out_d = out.rearrange("b (t p) d -> (b t) p d", p=P)
    w_in_d, w_up_d, w_down_d = w_in[0], w_up[0], w_down[0]
    b_up_d = b_up[0].rearrange("e (j n) -> (e j) n", n=CH)
    b_down_d = b_down[0].rearrange("e (j n) -> (e j) n", n=CF)
    skew = nc.dram_tensor("skew", [P, HEADS, 3 * WINDOW], F32, kind="Internal").ap()

    with ExitStack() as ctx:
        def sb(name, shape, dt=F32):
            return ctx.enter_context(nc.sbuf_tensor(name, shape, dt))

        def sem(name):
            return ctx.enter_context(nc.semaphore(name))

        ring = sb("ring", [P, R, SLOT])
        bank = [ctx.enter_context(nc.psum_tensor(f"bank{i}", [P, CH], F32)) for i in range(8)]

        acc = sb("acc", [P, TT, D])
        h_buf = sb("h_buf", [P, 2 * D])
        hT = h_buf[:, :].rearrange("p (k t) -> p k t", k=KD)
        x1r = h_buf[:, :].rearrange("p (t d) -> p t d", t=TT)
        m_buf = sb("m_buf", [P, 2 * D])
        xr = m_buf[:, :].rearrange("p (t d) -> p t d", t=TT)
        mixedT = m_buf[:, :].rearrange("p (k t) -> p k t", k=KD)
        hid = m_buf[:, 0:D]
        hidT = m_buf[:, D:2 * D].rearrange("p (k s) -> p k s", k=KD)
        u_buf = sb("u_buf", [P, NG * (PAD + SEQ)])
        uT = u_buf[:, :].rearrange("p (g t) -> p g t", g=NG)
        pooledT = u_buf[:, 0:NG * SEQ].rearrange("p (g t) -> p g t", g=NG)
        pick = u_buf[:, 0:2 * P].rearrange("p (t s) -> p t s", t=TT)
        spread = u_buf[:, 2 * P:4 * P].rearrange("p (t s) -> p t s", t=TT)
        spreadT = u_buf[:, 4 * P:6 * P]
        extra = u_buf[:, 6 * P:6 * P + 320]
        logits = u_buf[:, D:D + TT * E].rearrange("p (t e) -> p t e", t=TT)
        z_buf = sb("z_buf", [P, D])
        zT = z_buf[:, :].rearrange("p (g t) -> p g t", g=NG)
        attnT = z_buf[:, :].rearrange("p (k t) -> p k t", k=KW)
        xgT = z_buf[:, :].rearrange("p (k s) -> p k s", k=KD)
        vectors = z_buf[0:2 * KD + KW, 0:P]
        x1T = [b[:, 0:D].rearrange("p (k t) -> p k t", k=KD) for b in (u_buf, z_buf)]
        y = sb("y", [P, D])
        swi = sb("swi", [P, 3 * CF])
        glu, lin, sig = (swi[:, n * CF:(n + 1) * CF] for n in range(3))
        bmap = swi[0:N_BUCKETS + 1, 0:3 * WINDOW]
        route = swi[:, 0:6 * TT * E].rearrange("p (n t e) -> p n t e", n=6, t=TT)
        above, equal, count_eq, chosen, expd, dist_max = (route[:, n] for n in range(6))
        pw_buf = sb("pw_buf", [P, NG * P])
        pwt = pw_buf[:, :].rearrange("p (g d) -> p g d", g=NG)
        bup = pw_buf[:, 0:CH]
        row_buf = sb("row_buf", [P, NJ * P])
        ones, before = row_buf[:, 0:P], row_buf[:, P:2 * P]
        rows = row_buf[:, :].rearrange("p (j e s) -> p j e s", j=NJ, e=2)
        ident = sb("ident", [P, P])
        ids0 = sb("ids0", [P, SLOTS])
        ids = sb("ids", [P, SLOTS])
        ids_i = ids[:, :].bitcast(I32)
        rt_buf = sb("rt_buf", [P, KD * E])
        w_rt = rt_buf[:, :].rearrange("p (k e) -> p k e", k=KD)
        bdn = rt_buf[:, 0:CF]
        b_rt = sb("b_rt", [P, E])
        small = sb("small", [P, 128])
        vecT = small[:, 0:2 * KD + KW]
        g1, g2, psc = vecT[:, 0:KD], vecT[:, KD:2 * KD], vecT[:, 2 * KD:2 * KD + KW]
        ss, std, rstd = (small[:, 20 + 2 * n:22 + 2 * n] for n in range(3))
        eps, warm = small[:, 26:27], small[:, 27:28]
        snk = small[:, 28:36]
        inv_cnt = sb("inv_cnt", [P, NG, PAD])
        head = sb("head", [P, NG, PAD])
        stat = sb("stat", [P, 5, 2, HEADS])
        rank = sb("rank", [P, TT, E])
        gate = sb("gate", [P, TT, E])
        served = sb("served", [P, E])
        top = sb("top", [P, TT, 8])
        more = small[:, 36:36 + TT]
        late_bias = small[:, 38:38 + TT]
        gsum, ginv = small[:, 40:42], small[:, 42:44]
        rel = small[0:N_BUCKETS + 1, 44:44 + HEADS]
        fourths = small[:, 52:52 + TT * TOP_K].rearrange("p (t k) -> p t k", t=TT)
        ss_half = small[:, 60:60 + 2 * TT].rearrange("p (t h) -> p t h", t=TT)
        x_pair = sb("x_pair", [P, LISTED], I32)
        x_off = sb("x_off", [P, LISTED])
        n_extra = sb("n_extra", [P, 1], I32)
        bias_row = y[0:HEADS, 0:3 * WINDOW]

        scores1 = ring[:, 7, 0:2048].rearrange("p (h k) -> p h k", h=HEADS)
        scores0 = ring[:, 7, 2048:3072].rearrange("p (h k) -> p h k", h=HEADS)
        band = ring[:, 8, 0:2048].rearrange("p (h k) -> p h k", h=HEADS)
        qT = ring[:, 8, 2048:3072].rearrange("p (k t) -> p k t", k=KW)
        kT = ring[:, 8, 3072:3584].rearrange("p (k t) -> p k t", k=KV_HEADS)
        vv = ring[:, 8, 3584:3840].rearrange("p (t d) -> p t d", t=TT)
        probsT1 = ring[:, 9, 0:2048].rearrange("p (h k q) -> p h k q", h=HEADS, k=2)
        probsT0 = ring[:, 9, 2048:3072].rearrange("p (h q) -> p h q", h=HEADS)
        sums = [ring[:, 9, n * 1088:(n + 1) * 1088].rearrange("p (g t) -> p g t", g=NG) for n in range(2)]
        result = x1r
        fin_slot = ALL_LOADS % R
        fin_g = ring[:, fin_slot, 0:D]

        full = [sem(f"slot{i}_full") for i in range(R)]
        x_loaded = [sem("x0_loaded"), sem("x1_loaded")]
        vec_loaded, bias_in_loaded = sem("vec_loaded"), sem("bias_in_loaded")
        pw_loaded, sinks_loaded, router_loaded = sem("pw_loaded"), sem("sinks_loaded"), sem("router_loaded")
        bup_loaded, bdn_loaded, fin_loaded = sem("bup_loaded"), sem("bdn_loaded"), sem("fin_loaded")
        skew_written, band_loaded, stored = sem("skew_written"), sem("band_loaded"), sem("stored")
        consts = sem("consts")
        unit_done = sem("unit_done")
        emptied = {"dve": sem("emptied_by_dve"), "act": sem("emptied_by_act")}
        dve_step, act_step, pool_step = sem("dve_step"), sem("act_step"), sem("pool_step")
        std_ready, rstd_ready = sem("std_ready"), sem("rstd_ready")
        xr_ready, x1r_ready = sem("xr_ready"), sem("x1r_ready")
        summed = sem("summed")
        z_ready, negmax_ready = sem("z_ready"), sem("negmax_ready")
        exp_ready, probs_ready = sem("exp_ready"), sem("probs_ready")
        sig_ready, mixed_ready = sem("sig_ready"), sem("mixed_ready")
        centred, expd_ready = sem("centred"), sem("expd_ready")
        chosen_ready, gates_ready = sem("chosen_ready"), sem("gates_ready")
        extra_ready = sem("extra_ready")
        up_done = sem("up_done")
        glu_ready, lin_ready = sem("glu_ready"), sem("lin_ready")
        sigmoid_ready, gated_ready = sem("sigmoid_ready"), sem("gated_ready")
        hid_ready = sem("hid_ready")
        hidT_done, hidT_copied = sem("hidT_done"), sem("hidT_copied")
        down_done = sem("down_done")
        down0_done = sem("down0_done")
        even_landed = sem("even_landed")
        y0_copied, y1_copied = sem("y0_copied"), sem("y1_copied")
        ids_ready = sem("ids_ready")
        pick_ready, spread_ready, rows_ready = sem("pick_ready"), sem("spread_ready"), sem("rows_ready")
        gather_done, xg_copied = sem("gather_done"), sem("xg_copied")
        spreadT_done, spreadT_copied = sem("spreadT_done"), sem("spreadT_copied")
        scatter_done = sem("scatter_done")
        added = sem("added")
        result_ready = sem("result_ready")

        def emptied_at(name):
            n = UNIT[name]
            by = UNITS[n][1]
            return emptied[by], sum(b == by for _, b in UNITS[:n + 1])

        def load_at(n):
            return full[n % R], LANDED * (n // R + 1)

        up_banks, down_banks, turn_banks, scatter_banks = bank[0:2], bank[2:4], bank[4:6], bank[6:8]

        block = ctx.enter_context(nc.Block())

        @block.sync
        def _(sp):
            def load_w_in(n, c):
                wide = min(CH, w_in_d.shape[1] - c * CH)
                sp.dma_start(ring[:, n % R, 0:KD * wide].rearrange("p (k n) -> p k n", k=KD),
                             w_in_d[:, c * CH:c * CH + wide].rearrange("(k p) n -> p k n", p=P)).then_inc(full[n % R], LANDED)

            def load_rows(n, src):
                sp.dma_start(ring[:, n % R, :].rearrange("p (k n) -> p k n", n=D),
                             src.rearrange("(k p) n -> p k n", p=P)).then_inc(full[n % R], LANDED)

            def load_expert(slot, load, expert):
                dst = ring[:, slot, :]
                if load < UP_LOADS:
                    cols, half = slice(load // 2 * CH, (load // 2 + 1) * CH), slice(load % 2 * CH, (load % 2 + 1) * CH)
                    for e in range(2):
                        src = w_up_d[bass.ds(expert + e, 1), half, cols].rearrange("e (k p) n -> p (e k) n", p=P)
                        sp.dma_start(dst[:, e * SLOT // 2:(e + 1) * SLOT // 2].rearrange("p (k n) -> p k n", n=CH),
                                     src).then_inc(full[slot], LANDED // 2)
                else:
                    m = load - UP_LOADS
                    src = w_down_d[bass.ds(expert, 2), m * CF:(m + 1) * CF, :].rearrange("e (p k) n -> p e (k n)", p=P)
                    dst = dst.rearrange("p (e n) -> p e n", e=2)
                    if load < LOADS - 1:
                        sp.dma_start(dst, src).then_inc(full[slot], LANDED)
                    else:
                        sp.dma_start(dst[:, :, 0:D], src[:, :, 0:D]).then_inc(even_landed, 16)
                        sp.dma_start(dst[:, :, D:2 * D], src[:, :, D:2 * D]).then_inc(full[slot], LANDED)

            for t in range(TT):
                sp.dma_start(acc[:, t, :], x_d[t]).then_inc(x_loaded[t], 16)
            sp.dma_start(vectors[0:KD, :], norm1_g[0].rearrange("(k p) -> k p", p=P)).then_inc(vec_loaded, 16)
            sp.dma_start(vectors[KD:2 * KD, :], norm2_g[0].rearrange("(k p) -> k p", p=P)).then_inc(vec_loaded, 16)
            sp.dma_start(vectors[2 * KD:2 * KD + KW, :], pool_scale[0].rearrange("(k p) -> k p", p=P)).then_inc(vec_loaded, 16)
            for n in (C_U, C_KV, C_Q, C_GP):
                load_w_in(n, W_IN_LOAD.index(n))
            load_rows(W_POOL, w_pool_proj[0])
            load_w_in(C_GPA, W_IN_LOAD.index(C_GPA))
            load_rows(W_ATTN, w_attn_proj[0])
            sp.wait_ge(unit_done, UNIT["pool1"] + 1)
            sp.dma_start(bup, b_up_d).then_inc(bup_loaded, 16)
            sp.wait_ge(unit_done, UNIT["attn1"] + 1)
            load_w_in(C_GA, W_IN_LOAD.index(C_GA))
            load_w_in(C_GA2, W_IN_LOAD.index(C_GA2))
            load_rows(W_OUT0, w_out[0][0:CH, :])
            load_rows(W_OUT1, w_out[0][CH:D, :])
            last_use = ["gate_pool1", "q1", "gate_pool5", "gate_pool7", "gate_attn1", "gate_attn7",
                        "gate_attn5", "gate_attn7", "out3", "out3"]
            for load in range(LOADS):
                if load < R:
                    sp.wait_ge(unit_done, UNIT[last_use[load]] + 1)
                else:
                    sp.wait_ge(up_done, load - R + 1)
                load_expert((MIXER_LOADS + load) % R, load, 0)

            def wait_freed(g, load):
                back, g0 = load - R, 0
                if back < 0:
                    back, g0 = back + LOADS, -1
                if back < UP_LOADS:
                    sp.wait_ge(up_done, UP_LOADS * (g + g0) + (back + 1))
                else:
                    sp.wait_ge(down_done, 4 * (g + g0) + (back - UP_LOADS + 1))

            with sp.Fori(0, (PASSES - 1) // UNROLL) as i:
                for q in range(UNROLL):
                    g = i * UNROLL + (q + 1)
                    for load in range(LOADS):
                        wait_freed(g, load)
                        load_expert((MIXER_LOADS + (q + 1) * LOADS + load) % R, load, g * 2)

            sp.wait_ge(extra_ready, 1)
            extras = sp.value_load(n_extra[0:1, 0:1], min_val=0, max_val=LISTED)
            with sp.If(extras > 0):
                with sp.Fori(0, extras) as t:
                    pair = sp.value_load(x_pair[0:1, bass.ds(t, 1)], min_val=0, max_val=PASSES - 1)
                    for load in range(LOADS):
                        if load < R:
                            sp.wait_ge(down_done, (t + PASSES) * 4)
                        else:
                            sp.wait_ge(up_done, (t + PASSES) * UP_LOADS + (load - R + 1))
                        load_expert((ALL_LOADS + load - LOADS) % R, load, pair * 2)
            with sp.Else():
                pass
            sp.wait_ge(up_done, (extras + PASSES) * UP_LOADS - (UP_LOADS - 3))
            sp.dma_start(fin_g, final_g.partition_broadcast(P)).then_inc(fin_loaded, 16)
            sp.wait_ge(result_ready, 1)
            sp.dma_start(out_d[0], result[:, 0, :]).then_inc(stored, 16)
            for n in range(2):
                sp.wait_ge(result_ready, n + 2)
                sp.dma_start(out_d[1][:, n * CH:(n + 1) * CH], result[:, 1, n * CH:(n + 1) * CH]).then_inc(stored, 16)
            sp.wait_ge(stored, 16 * 3)

        @block.gpsimd
        def _(pool):
            nc.gpsimd.memset(rel[N_BUCKETS:N_BUCKETS + 1, :], 1.0).then_inc(consts, 1)
            pool.wait_ge(consts, 1)
            nc.gpsimd.memset(ident[:, :], 0.0).then_inc(consts, 1)
            nc.gpsimd.memset(eps, EPS).then_inc(consts, 1)
            pool.wait_ge(consts, 2)
            nc.gpsimd.affine_select(out=ident[:, :], in_=ident[:, :], compare_op=ALU.not_equal, fill=1.0,
                                    base=0, pattern=[[-1, P]], channel_multiplier=1).then_inc(consts, 1)
            nc.gpsimd.memset(uT[:, :, 0:PAD], 0.0).then_inc(consts, 1)
            for s in sums:
                nc.gpsimd.memset(s[:, :, 0:PAD], 0.0).then_inc(consts, 1)
            nc.gpsimd.memset(ones, 1.0).then_inc(consts, 1)
            nc.gpsimd.iota(ids_i, pattern=[[1, SLOTS]], base=0, channel_multiplier=0).then_inc(consts, 1)
            pool.wait_ge(consts, 8)
            nc.gpsimd.affine_select(out=before, in_=ones, compare_op=ALU.is_gt, fill=0.0,
                                    base=0, pattern=[[1, P]], channel_multiplier=-1).then_inc(consts, 1)
            pool.wait_ge(*emptied_at("bias_rows"))
            src = bias_row.unsqueeze(1).broadcast_to([HEADS, P, 3 * WINDOW])
            nc.gpsimd.dma_start(skew.rearrange("p h i -> h p i"), src).then_inc(skew_written, 16)
            src = uT
            for step in range(NG):
                if step == 0:
                    pool.wait_ge(*emptied_at("u1"))
                else:
                    pool.wait_ge(summed, step)
                dst, far = sums[step % 2], 1 << step
                nc.gpsimd.tensor_tensor(dst[:, step:NG, PAD:], src[:, step:NG, PAD:],
                                        src[:, step:NG, PAD - far:PAD + SEQ - far], ALU.add).then_inc(summed, 1)
                src = dst
            pool.wait_ge(skew_written, 16)
            pitch = HEADS * 3 * WINDOW
            back = bass.AP(skew.tensor, WINDOW - 1, [[pitch - 1, P], [3 * WINDOW, HEADS], [1, 2 * WINDOW]])
            nc.gpsimd.dma_start(band, back).then_inc(band_loaded, 16)

        @block.scalar
        def _(act):
            act.dma_start(rel[0:N_BUCKETS, :], rel_bias).then_inc(bias_in_loaded, 16)
            act.dma_start(bmap, buckets).then_inc(bias_in_loaded, 16)
            act.dma_start(pwt, pool_w[0].rearrange("g c d -> c g d")).then_inc(pw_loaded, 16)
            act.dma_start(snk, sinks[0].partition_broadcast(P)).then_inc(sinks_loaded, 16)
            act.dma_start(w_rt, w_router[0].rearrange("(k p) e -> p k e", p=P)).then_inc(router_loaded, 16)
            act.dma_start(b_rt[:, :], b_router[0].partition_broadcast(P)).then_inc(router_loaded, 16)

            steps = [0]

            def link(ins):
                steps[0] += 1
                ins.then_inc(act_step, 1)
                act.wait_ge(act_step, steps[0])

            act.wait_ge(consts, 3)
            for t in range(TT):
                act.wait_ge(x_loaded[t], 16)
                link(nc.scalar.activation(xr[:, t, :], acc[:, t, :], ACT.Square, accum_out=ss[:, t:t + 1]))
                nc.scalar.activation(std[:, t:t + 1], ss[:, t:t + 1], ACT.Sqrt, bias=eps,
                                     scale=1.0 / D).then_inc(std_ready, 1)
            for i in range(2):
                act.wait_ge(unit_done, UNIT[f"q{i}"] + 1)
                nc.scalar.mul(qT[:, 2 * i:2 * i + 2, :].rearrange("p k t -> p (k t)"), bank[UNIT[f"q{i}"] % 8][:, :],
                              HD ** -0.5).then_inc(emptied["act"], 1)
            for i in range(2):
                act.wait_ge(unit_done, UNIT[f"pool{i}"] + 1)
                for g in (2 * i, 2 * i + 1):
                    ins = nc.scalar.activation(pooledT[:, g, :], bank[UNIT[f"pool{i}"] % 8][:, (g % 2) * SEQ:(g % 2 + 1) * SEQ],
                                               ACT.Copy, scale=psc[:, g:g + 1])
                ins.then_inc(emptied["act"], 1)
            act.wait_ge(negmax_ready, 1)
            for b, s in enumerate((scores0, scores1)):
                for h in range(HEADS):
                    nc.scalar.activation(s[:, h, :], s[:, h, :], ACT.Exp, bias=stat[:, 1, b, h:h + 1],
                                         accum_out=stat[:, 3, b, h:h + 1])
            nc.scalar.activation(stat[:, 2], stat[:, 2], ACT.Exp).then_inc(exp_ready, 1)
            gates = [f"gate_pool{c}" for c in range(KD)] + [f"gate_attn{c}" for c in range(KD)]

            def gate_sigmoid(n):
                u = UNIT[gates[n]]
                act.wait_ge(unit_done, u + 1)
                if n >= 2:
                    act.wait_ge(*emptied_at(gates[n - 2]))
                nc.scalar.activation(swi[:, (n % 2) * CF:(n % 2 + 1) * CF], bank[u % 8][:, 0:SEQ],
                                     ACT.Sigmoid).then_inc(sig_ready, 1)
            for c in range(KD - 1):
                gate_sigmoid(c)
            for i in range(1, 6, 2):
                u = UNIT[f"probsT{i}"]
                act.wait_ge(unit_done, u + 1)
                dst = probsT1[:, 2 * i:2 * i + 2] if i < 4 else probsT0[:, 4 * (i - 4):4 * (i - 4) + 4]
                dst = dst.rearrange("p h k q -> p (h k q)") if i < 4 else dst.rearrange("p h q -> p (h q)")
                nc.scalar.copy(dst, bank[u % 8][:, :]).then_inc(emptied["act"], 1)
            for c in range(KD - 1, 2 * KD):
                gate_sigmoid(c)
            link(nc.scalar.activation(warm, eps, ACT.Sqrt))
            for t in range(TT):
                act.wait_ge(*emptied_at(f"out{2 * t + 1}"))
                link(nc.scalar.activation(x1r[:, t, :], acc[:, t, :], ACT.Square, accum_out=ss[:, t:t + 1]))
                nc.scalar.activation(std[:, t:t + 1], ss[:, t:t + 1], ACT.Sqrt, bias=eps,
                                     scale=1.0 / D).then_inc(std_ready, 1)
                act.wait_ge(rstd_ready, TT + t + 1)
                nc.scalar.activation(x1r[:, t, :], acc[:, t, :], ACT.Copy, scale=rstd[:, t:t + 1]).then_inc(x1r_ready, 1)
            link(nc.scalar.activation(warm, eps, ACT.Exp))
            act.wait_ge(unit_done, UNIT["logits1"] + 1)
            act.dma_start(bdn, b_down_d).then_inc(bdn_loaded, 16)
            act.wait_ge(centred, 1)
            nc.scalar.activation(expd, dist_max, ACT.Exp).then_inc(expd_ready, 1)
            link(nc.scalar.activation(warm, eps, ACT.Sigmoid))

            def copy_spreadT(g):
                act.wait_ge(spreadT_done, g + 1)
                nc.scalar.copy(spreadT, up_banks[0][:, 0:SEQ]).then_inc(spreadT_copied, 1)

            def copy_hidT(g, j):
                act.wait_ge(hidT_done, g * NJ + (j + 1))
                nc.scalar.copy(hidT[:, 2 * j:2 * j + 2, :].rearrange("p k s -> p (k s)"),
                               turn_banks[j % 2][:, 0:2 * P]).then_inc(hidT_copied, 1)

            def act_pass(g):
                for j in range(NJ):
                    act.wait_ge(glu_ready, g * NJ + (j + 1))
                    nc.scalar.activation(sig, glu, ACT.Sigmoid, scale=ALPHA).then_inc(sigmoid_ready, 1)
                    if j >= 1:
                        copy_hidT(g, j - 1)
                copy_hidT(g, NJ - 1)
                act.wait_ge(down0_done, g + 1)
                nc.scalar.copy(y[:, 0:CH], down_banks[0][:, :]).then_inc(y0_copied, 1)

            copy_spreadT(0)
            with act.Fori(0, PASSES - 1) as g:
                act_pass(g)
                copy_spreadT(g + 1)
            act_pass(PASSES - 1)
            act.wait_ge(extra_ready, 1)
            extras = act.value_load(n_extra[0:1, 0:1], min_val=0, max_val=LISTED)
            with act.If(extras > 0):
                with act.Fori(0, extras) as t:
                    copy_spreadT(t + PASSES)
                    act_pass(t + PASSES)
            with act.Else():
                pass
            link(nc.scalar.activation(warm, eps, ACT.Sqrt))
            for t in range(TT):
                for n in range(2):
                    act.wait_ge(added, (extras + PASSES) * 4 + (2 * t + n - 3))
                    link(nc.scalar.activation(xr[:, t, n * CH:(n + 1) * CH], acc[:, t, n * CH:(n + 1) * CH], ACT.Square,
                                              accum_out=ss_half[:, t, n:n + 1]))
                    if n == 0:
                        link(nc.scalar.activation(late_bias[:, t:t + 1], ss_half[:, t, 0:1], ACT.Identity, bias=eps,
                                                  scale=1.0 / D))
                nc.scalar.activation(std[:, t:t + 1], ss_half[:, t, 1:2], ACT.Sqrt, bias=late_bias[:, t:t + 1],
                                     scale=1.0 / D).then_inc(std_ready, 1)

        @block.tensor
        def _(pe):
            def begin(name):
                n = UNIT[name]
                if n >= 8:
                    pe.wait_ge(*emptied_at(UNITS[n - 8][0]))
                return bank[n % 8]

            pe.wait_ge(vec_loaded, 48)
            pe.wait_ge(consts, 4)
            b = begin("vectors")
            nc.tensor.transpose(b[:, 0:2 * KD + KW], vectors, ident[0:2 * KD + KW, 0:2 * KD + KW]).then_inc(unit_done, 1)
            pe.wait_ge(bias_in_loaded, 32)
            b = begin("bias_rows")
            nc.tensor.matmul(b[0:HEADS, 0:3 * WINDOW], rel, bmap, start=True, stop=True).then_inc(unit_done, 1)
            for m in range(4):
                b = begin(f"xT{m}")
                for k in (2 * m, 2 * m + 1):
                    for t in range(TT):
                        if m == 0 and k == 0:
                            pe.wait_ge(xr_ready, t + 1)
                        ins = nc.tensor.transpose(b[:, (k % 2) * SEQ + t * P:(k % 2) * SEQ + (t + 1) * P],
                                                  xr[:, t, k * P:(k + 1) * P], ident[:, :])
                ins.then_inc(unit_done, 1)

            def chunk(n, wide=CH):
                return ring[:, n % R, 0:KD * wide].rearrange("p (k n) -> p k n", k=KD)

            def project(dst, w, c, rhs, kn):
                for k in range(kn):
                    ins = nc.tensor.matmul(dst, w[:, k, c * P:(c + 1) * P], rhs[:, k, :], start=(k == 0), stop=(k == kn - 1))
                return ins

            pe.wait_ge(*load_at(C_U))
            pe.wait_ge(*emptied_at("xT3"))
            for i in range(2):
                b = begin(f"u{i}")
                for c in (2 * i, 2 * i + 1):
                    ins = project(b[:, (c % 2) * SEQ:(c % 2 + 1) * SEQ], chunk(C_U), c, hT, KD)
                ins.then_inc(unit_done, 1)
            pe.wait_ge(*load_at(C_KV))
            b = begin("kv")
            project(b[:, 0:SEQ], chunk(C_KV), 0, hT, KD)
            for t in range(TT):
                for k in range(KD):
                    ins = nc.tensor.matmul(b[:, SEQ + t * P:SEQ + (t + 1) * P], hT[:, k, t * P:(t + 1) * P],
                                           chunk(C_KV)[:, k, P:2 * P], start=(k == 0), stop=(k == KD - 1))
            ins.then_inc(unit_done, 1)
            pe.wait_ge(*load_at(C_Q))
            for i in range(2):
                b = begin(f"q{i}")
                for c in (2 * i, 2 * i + 1):
                    ins = project(b[:, (c % 2) * SEQ:(c % 2 + 1) * SEQ], chunk(C_Q), c, hT, KD)
                ins.then_inc(unit_done, 1)
            pe.wait_ge(pw_loaded, 16)
            pe.wait_ge(z_ready, 1)
            for i in range(2):
                b = begin(f"pool{i}")
                for g in (2 * i, 2 * i + 1):
                    ins = nc.tensor.matmul(b[:, (g % 2) * SEQ:(g % 2 + 1) * SEQ], pwt[:, g, :], zT[:, g, :], start=True, stop=True)
                ins.then_inc(unit_done, 1)
            pe.wait_ge(*emptied_at("q1"))
            pe.wait_ge(*emptied_at("kv"))
            for blk, keys, groups in ((1, 2 * WINDOW, ((0, 1, 2, 3), (4, 5, 6, 7))), (0, WINDOW, (tuple(range(8)),))):
                for n, hs in enumerate(groups):
                    bs = [begin(f"scores{blk}_{2 * n + odd}") for odd in range(2)]
                    for at, h in enumerate(hs):
                        lo = HD * (h % 2)
                        ins = nc.tensor.matmul(bs[h % 2][:, (at // 2) * keys:(at // 2 + 1) * keys],
                                               qT[lo:lo + HD, h // 2, blk * P:(blk + 1) * P],
                                               kT[lo:lo + HD, h // 4, 0:keys], start=True, stop=True)
                        if at >= len(hs) - 2:
                            ins.then_inc(unit_done, 1)
            def gated(kind, at, w_load, rhs, channels, rhs_ready):
                for c in channels:
                    n = W_IN_LOAD[(at + c * P) // CH]
                    pe.wait_ge(*load_at(n))
                    wide = CH if n != C_GA2 else CH // 2
                    b = begin(f"{kind}{c}")
                    project(b[:, 0:SEQ], chunk(n, wide), (at + c * P) % CH // P, hT, KD)
                    if c == 0:
                        pe.wait_ge(*load_at(w_load))
                        pe.wait_ge(*emptied_at(rhs_ready))
                    w = ring[:, w_load % R, :].rearrange("p (k n) -> p k n", n=D)
                    project(b[:, SEQ:2 * SEQ], w, c, rhs, KW).then_inc(unit_done, 1)

            gated("gate_pool", GATE_POOL_AT, W_POOL, pooledT, range(KD - 1), "pool1")
            for i in range(6):
                b = begin(f"probsT{i}")
                if i == 0:
                    pe.wait_ge(probs_ready, 1)
                for n in range(4):
                    if i < 4:
                        src = scores1[:, 2 * i + n // 2, (n % 2) * P:(n % 2 + 1) * P]
                    else:
                        src = scores0[:, 4 * (i - 4) + n, :]
                    ins = nc.tensor.transpose(b[:, n * P:(n + 1) * P], src, ident[:, :])
                ins.then_inc(unit_done, 1)
            gated("gate_pool", GATE_POOL_AT, W_POOL, pooledT, [KD - 1], "pool1")
            for i in range(2):
                b = begin(f"attn{i}")
                if i == 0:
                    pe.wait_ge(*emptied_at("probsT4"))
                    pe.wait_ge(*emptied_at("probsT5"))
                for hp in (2 * i, 2 * i + 1):
                    at = (hp % 2) * SEQ
                    for blk, kt in ((0, 0), (1, 0), (1, 1)):
                        for h in (2 * hp, 2 * hp + 1):
                            lo = HD * (h % 2)
                            rhs = probsT1[:, h, kt, :] if blk else probsT0[:, h, :]
                            ins = nc.tensor.matmul(b[lo:lo + HD, at + blk * P:at + (blk + 1) * P],
                                                   vv[:, kt, HD * (h // 4):HD * (h // 4 + 1)], rhs,
                                                   start=(kt == 0), stop=(blk == kt))
                ins.then_inc(unit_done, 1)
            gated("gate_attn", GATE_ATTN_AT, W_ATTN, attnT, range(KD), "attn1")

            def out_unit(q):
                t, n = q // 2, q % 2
                b = begin(f"out{q}")
                for k in range(KD):
                    if q == 0:
                        pe.wait_ge(mixed_ready, k + 1)
                    w = ring[:, (W_OUT0 + k // 4) % R, :].rearrange("p (k n) -> p k n", n=D)
                    ins = nc.tensor.matmul(b[:, :], mixedT[:, k, t * P:(t + 1) * P], w[:, k % 4, n * CH:(n + 1) * CH],
                                           start=(k == 0), stop=(k == KD - 1))
                ins.then_inc(unit_done, 1)

            def turn_x1(t, half):
                pe.wait_ge(*emptied_at(f"out{2 * t + half}"))
                b = begin(f"x1T{2 * t + half}")
                for k in range(4):
                    ins = nc.tensor.transpose(b[:, k * P:(k + 1) * P],
                                              acc[:, t, (4 * half + k) * P:(4 * half + k + 1) * P], ident[:, :])
                ins.then_inc(unit_done, 1)

            def logits_part(b, t, half):
                pe.wait_ge(*emptied_at(f"x1T{2 * t + half}"))
                for k in range(4 * half, 4 * half + 4):
                    ins = nc.tensor.matmul(b[:, 0:E], x1T[t][:, k, :], w_rt[:, k, :], start=(k == 0), stop=(k == KD - 1))
                return ins

            pe.wait_ge(*load_at(W_OUT0))
            pe.wait_ge(*load_at(W_OUT1))
            pe.wait_ge(router_loaded, 32)
            for q in range(3):
                out_unit(q)
            for half in range(2):
                turn_x1(0, half)
            b = begin("logits0")
            logits_part(b, 0, 0)
            logits_part(b, 0, 1).then_inc(unit_done, 1)
            turn_x1(1, 0)
            out_unit(3)
            b = begin("logits1")
            logits_part(b, 1, 0)
            turn_x1(1, 1)
            logits_part(b, 1, 1).then_inc(unit_done, 1)
            pe.wait_ge(consts, 10)
            pe.wait_ge(chosen_ready, 1)
            b = begin("ranks")
            nc.tensor.matmul(b[:, 0:E], before, chosen[:, 0, :], start=True, stop=True)
            nc.tensor.matmul(b[:, E:2 * E], ones, chosen[:, 0, :], start=True, stop=False)
            pe.wait_ge(chosen_ready, TT)
            nc.tensor.matmul(b[:, E:2 * E], before, chosen[:, 1, :], start=False, stop=True).then_inc(unit_done, 1)
            b = begin("served")
            nc.tensor.matmul(b[:, 0:E], ones, chosen[:, 0, :], start=True, stop=False)
            nc.tensor.matmul(b[:, 0:E], ones, chosen[:, 1, :], start=False, stop=True).then_inc(unit_done, 1)

            def gather(g, half):
                pe.wait_ge(pick_ready, g + 1)
                for k in range(4 * half, 4 * half + 4):
                    for t in range(TT):
                        ins = nc.tensor.matmul(turn_banks[k // 4][:, (k % 4) * P:(k % 4 + 1) * P], x1r[:, t, k * P:(k + 1) * P],
                                               pick[:, t, :], start=(t == 0), stop=(t == TT - 1))
                    if k % 4 == 3:
                        ins.then_inc(gather_done, 1)

            def turn_spread(g):
                pe.wait_ge(spread_ready, g + 1)
                for t in range(TT):
                    ins = nc.tensor.transpose(up_banks[0][:, t * P:(t + 1) * P], spread[:, t, :], ident[:, :])
                ins.then_inc(spreadT_done, 1)

            def turn_hid(g, j):
                pe.wait_ge(hid_ready, g * NJ + (j + 1))
                if j >= 2:
                    pe.wait_ge(hidT_copied, g * NJ + (j - 1))
                for c in range(2):
                    ins = nc.tensor.transpose(turn_banks[j % 2][:, c * P:(c + 1) * P],
                                              hid[:, j * CF + c:(j + 1) * CF:2], ident[:, :])
                ins.then_inc(hidT_done, 1)

            def pe_pass(g, slot_load, last_slot, following):
                def up_bias(j):
                    nc.tensor.matmul(up_banks[j % 2][:, :], rows[:, j].rearrange("p e s -> p (e s)"), bup, start=True,
                                     stop=False, skip_group_check=True)

                for j in range(NJ):
                    b = up_banks[j % 2]
                    if j == 0:
                        pe.wait_ge(spreadT_copied, g + 1)
                        pe.wait_ge(rows_ready, g + 1)
                    if j != 1:
                        up_bias(j)
                    for half in range(2):
                        if j == 0 and half == 1:
                            gather(g, 1)
                            up_bias(1)
                        if j == 0:
                            pe.wait_ge(xg_copied, g * 2 + (half + 1))
                        w = slot_load(2 * j + half).rearrange("p (e k n) -> p e k n", e=2, n=CH)
                        for k in range(4):
                            at = 4 * half + k
                            for e in range(2):
                                ins = nc.tensor.matmul(b[e * SLOTS:(e + 1) * SLOTS, :], xgT[:, at, e * SLOTS:(e + 1) * SLOTS],
                                                       w[:, e, k, :], start=False, stop=(at == KD - 1), skip_group_check=True)
                        ins.then_inc(up_done, 1)
                    if j >= 1:
                        turn_hid(g, j - 1)
                pe.wait_ge(bdn_loaded, 16)
                for n in range(2):
                    for c in range(2):
                        nc.tensor.matmul(down_banks[n][:, c * CF:(c + 1) * CF], rows[:, 2 * n + c].rearrange("p e s -> p (e s)"),
                                         bdn, start=(c == 0), stop=False, skip_group_check=True)
                for m in range(4):
                    pe.wait_ge(hidT_copied, g * NJ + (m + 1))
                    for k in (2 * m, 2 * m + 1):
                        if k == KD - 2:
                            pe.wait_ge(even_landed, g * 16 + 16)
                            w = last_slot.rearrange("p (e k n) -> p e k n", e=2, n=D)
                        elif k % 2 == 0 or k == KD - 1:
                            w = slot_load(UP_LOADS + m).rearrange("p (e k n) -> p e k n", e=2, n=D)
                        for n in range(2):
                            for e in range(2):
                                ins = nc.tensor.matmul(down_banks[n][e * SLOTS:(e + 1) * SLOTS, :],
                                                       hidT[:, k, e * SLOTS:(e + 1) * SLOTS],
                                                       w[:, e, k % 2, n * CH:(n + 1) * CH],
                                                       start=False, stop=(k == KD - 1), skip_group_check=True)
                            if k == KD - 1 and n == 0:
                                ins.then_inc(down0_done, 1)
                    ins.then_inc(down_done, 1)
                    if m == 1:
                        turn_hid(g, NJ - 1)
                if following:
                    gather(g + 1, 0)
                for q in range(4):
                    t, n = q // 2, q % 2
                    if q < 2:
                        pe.wait_ge((y0_copied, y1_copied)[q], g + 1)
                    if q >= 2:
                        pe.wait_ge(added, g * 4 + (q - 1))
                    nc.tensor.matmul(scatter_banks[q % 2][:, :], spreadT[:, t * P:(t + 1) * P], y[:, n * CH:(n + 1) * CH],
                                     start=True, stop=True).then_inc(scatter_done, 1)
                if following:
                    turn_spread(g + 1)

            pe.wait_ge(x1r_ready, TT)
            gather(0, 0)
            turn_spread(0)
            pe.wait_ge(bup_loaded, 16)

            def main_slot(i, q):
                def slot_load(load):
                    n = MIXER_LOADS + q * LOADS + load
                    pe.wait_ge(full[n % R], i * (LANDED * UNROLL * LOADS // R) + LANDED * (n // R + 1))
                    return ring[:, n % R, :]
                return slot_load

            def last_slot(q):
                return ring[:, (MIXER_LOADS + (q + 1) * LOADS - 1) % R, :]

            with pe.Fori(0, (PASSES - 1) // UNROLL) as i:
                for q in range(UNROLL):
                    pe_pass(i * UNROLL + q, main_slot(i, q), last_slot(q), True)
            pe_pass(PASSES - 1, main_slot((PASSES - 1) // UNROLL, 0), last_slot(0), False)

            pe.wait_ge(extra_ready, 1)
            extras = pe.value_load(n_extra[0:1, 0:1], min_val=0, max_val=LISTED)
            extra_slots = [(ALL_LOADS + load - LOADS) % R for load in range(LOADS)]
            with pe.If(extras > 0):
                with pe.Fori(0, extras) as t:
                    def slot_load(load):
                        slot = extra_slots[load]
                        landed = len(range(slot, ALL_LOADS, R))
                        pe.wait_ge(full[slot], t * (LANDED * extra_slots.count(slot))
                                   + LANDED * (landed + extra_slots[:load + 1].count(slot)))
                        return ring[:, slot, :]
                    gather(t + PASSES, 0)
                    turn_spread(t + PASSES)
                    pe_pass(t + PASSES, slot_load, ring[:, extra_slots[-1], :], False)
            with pe.Else():
                pass

        @block.vector
        def _(dve):
            steps = [0]

            def link(ins):
                steps[0] += 1
                ins.then_inc(dve_step, 1)
                dve.wait_ge(dve_step, steps[0])

            def unit(name):
                dve.wait_ge(unit_done, UNIT[name] + 1)
                return bank[UNIT[name] % 8]

            def empties(ins):
                ins.then_inc(emptied["dve"], 1)

            def invert_std(t, first):
                dve.wait_ge(std_ready, first + t + 1)
                nc.vector.reciprocal(rstd[:, t:t + 1], std[:, t:t + 1]).then_inc(rstd_ready, 1)

            b = unit("vectors")
            empties(nc.vector.tensor_copy(vecT, b[:, 0:2 * KD + KW]))
            b = unit("bias_rows")
            empties(nc.vector.tensor_copy(bias_row, b[0:HEADS, 0:3 * WINDOW]))
            dve.wait_ge(consts, 9)
            link(nc.vector.tensor_copy(ids0[:, :], ids_i))
            for g, w in enumerate(POOL_WINDOWS):
                ins = nc.vector.tensor_scalar(inv_cnt[:, g, :], ids0[:, 0:PAD], 1.0, float(w), ALU.add, ALU.min)
            link(ins)
            link(nc.vector.reciprocal(inv_cnt[:, :, :], inv_cnt[:, :, :]))
            link(nc.vector.tensor_scalar(ids0[:, :], ids0[:, :], -UNRANKED, None, ALU.add))
            link(nc.vector.tensor_copy(ids[:, :], ids0[:, :]))
            for t in range(TT):
                invert_std(t, 0)
                dve.wait_ge(rstd_ready, t + 1)
                nc.vector.tensor_scalar(xr[:, t, :], acc[:, t, :], rstd[:, t:t + 1], None, ALU.mult).then_inc(xr_ready, 1)
            dve.wait_ge(*emptied_at("vectors"))
            for m in range(4):
                b = unit(f"xT{m}")
                empties(nc.vector.tensor_tensor(hT[:, 2 * m:2 * m + 2, :], b[:, :].rearrange("p (k t) -> p k t", k=2),
                                                g1[:, 2 * m:2 * m + 2].unsqueeze(2).broadcast_to([P, 2, SEQ]), ALU.mult))
            dve.wait_ge(consts, 7)
            for i in range(2):
                b = unit(f"u{i}")
                empties(nc.vector.tensor_copy(uT[:, 2 * i:2 * i + 2, PAD:], b[:, :].rearrange("p (g t) -> p g t", g=2)))
            b = unit("kv")
            for kv in range(KV_HEADS):
                for half in range(2):
                    nc.vector.tensor_copy(kT[half * HD:(half + 1) * HD, kv, :], b[kv * HD:(kv + 1) * HD, 0:SEQ])
            empties(nc.vector.tensor_copy(vv.rearrange("p t d -> p (t d)"), b[:, SEQ:2 * SEQ]))
            dve.wait_ge(summed, NG)
            dve.wait_ge(*emptied_at("u1"))
            for g, w in enumerate(POOL_WINDOWS):
                nc.vector.scalar_tensor_tensor(zT[:, g, :], sums[g % 2][:, g, PAD:], 1.0 / w, uT[:, g, PAD:], ALU.mult, ALU.subtract)
                ins = nc.vector.tensor_tensor(head[:, g, :], sums[g % 2][:, g, PAD:2 * PAD], inv_cnt[:, g, :], ALU.mult)
            link(ins)
            nc.vector.tensor_tensor(zT[:, :, 0:PAD], head[:, :, :], uT[:, :, PAD:2 * PAD], ALU.subtract).then_inc(z_ready, 1)
            dve.wait_ge(band_loaded, 16)
            for n in range(4):
                b = unit(f"scores1_{n}")
                h0 = 4 * (n // 2) + n % 2
                empties(nc.vector.tensor_tensor(scores1[:, h0:h0 + 3:2, :], b[:, :].rearrange("p (h k) -> p h k", h=2),
                                                band[:, h0:h0 + 3:2, :], ALU.add))
            for n in range(2):
                b = unit(f"scores0_{n}")
                empties(nc.vector.tensor_tensor(scores0[:, n:HEADS:2, :], b[:, :].rearrange("p (h k) -> p h k", h=4),
                                                band[:, n:HEADS:2, WINDOW:], ALU.add))
            dve.wait_ge(sinks_loaded, 16)
            dve.wait_ge(*emptied_at("scores0_1"))
            nc.vector.tensor_reduce(stat[:, 0, 0, :], scores0, AX.X, ALU.max)
            link(nc.vector.tensor_reduce(stat[:, 0, 1, :], scores1, AX.X, ALU.max))
            sink2 = snk.unsqueeze(1).broadcast_to([P, 2, HEADS])
            link(nc.vector.tensor_tensor(stat[:, 0], stat[:, 0], sink2, ALU.max))
            nc.vector.tensor_tensor(stat[:, 2], sink2, stat[:, 0], ALU.subtract)
            nc.vector.tensor_scalar(stat[:, 1], stat[:, 0], -1.0, None, ALU.mult).then_inc(negmax_ready, 1)
            dve.wait_ge(exp_ready, 1)
            link(nc.vector.tensor_tensor(stat[:, 3], stat[:, 3], stat[:, 2], ALU.add))
            link(nc.vector.reciprocal(stat[:, 4], stat[:, 3]))
            nc.vector.tensor_tensor(scores0, scores0, stat[:, 4, 0, :].unsqueeze(2).broadcast_to([P, HEADS, WINDOW]), ALU.mult)
            nc.vector.tensor_tensor(scores1, scores1, stat[:, 4, 1, :].unsqueeze(2).broadcast_to([P, HEADS, 2 * WINDOW]),
                                    ALU.mult).then_inc(probs_ready, 1)

            def gated(kind, c, n):
                b = unit(f"{kind}{c}")
                dve.wait_ge(sig_ready, n + 1)
                s = swi[:, (n % 2) * CF:(n % 2 + 1) * CF]
                if kind == "gate_pool":
                    empties(nc.vector.tensor_tensor(mixedT[:, c, :], s, b[:, SEQ:2 * SEQ], ALU.mult))
                else:
                    if c >= 1:
                        dve.wait_ge(mixed_ready, c)
                    empties(nc.vector.tensor_tensor(swi[:, 2 * CF:3 * CF], s, b[:, SEQ:2 * SEQ], ALU.mult))
                    dve.wait_ge(*emptied_at(f"{kind}{c}"))
                    nc.vector.tensor_tensor(mixedT[:, c, :], mixedT[:, c, :], swi[:, 2 * CF:3 * CF], ALU.add).then_inc(mixed_ready, 1)

            for c in range(KD - 1):
                gated("gate_pool", c, c)
            for i in range(0, 6, 2):
                b = unit(f"probsT{i}")
                dst = probsT1[:, 2 * i:2 * i + 2] if i < 4 else probsT0[:, 4 * (i - 4):4 * (i - 4) + 4]
                dst = dst.rearrange("p h k q -> p (h k q)") if i < 4 else dst.rearrange("p h q -> p (h q)")
                empties(nc.vector.tensor_copy(dst, b[:, :]))
            gated("gate_pool", KD - 1, KD - 1)
            for i in range(2):
                b = unit(f"attn{i}")
                empties(nc.vector.tensor_copy(attnT[:, 2 * i:2 * i + 2, :].rearrange("p k t -> p (k t)"), b[:, :]))
            for c in range(KD):
                gated("gate_attn", c, KD + c)
            def add_out(q):
                t, n = q // 2, q % 2
                b = unit(f"out{q}")
                empties(nc.vector.tensor_tensor(acc[:, t, n * CH:(n + 1) * CH], acc[:, t, n * CH:(n + 1) * CH], b[:, :], ALU.add))

            def copy_x1T(t, half):
                b = unit(f"x1T{2 * t + half}")
                empties(nc.vector.tensor_tensor(x1T[t][:, 4 * half:4 * half + 4, :], b[:, :].rearrange("p (k t) -> p k t", k=4),
                                                g2[:, 4 * half:4 * half + 4].unsqueeze(2).broadcast_to([P, 4, P]), ALU.mult))

            def choose(t):
                invert_std(t, TT)
                dve.wait_ge(rstd_ready, TT + t + 1)
                b = unit(f"logits{t}")
                empties(nc.vector.scalar_tensor_tensor(logits[:, t, :], b[:, 0:E], rstd[:, t:t + 1], b_rt[:, :], ALU.mult, ALU.add))
                dve.wait_ge(*emptied_at(f"logits{t}"))
                link(nc.vector.max(top[:, t, :], logits[:, t, :]))

                fourth = top[:, t, TOP_K - 1:TOP_K]
                nc.vector.tensor_tensor(fourths[:, t, :], top[:, t, 0:TOP_K], fourth.broadcast_to([P, TOP_K]), ALU.is_equal)
                nc.vector.tensor_tensor(above[:, t, :], logits[:, t, :], fourth.broadcast_to([P, E]), ALU.is_gt)
                link(nc.vector.tensor_tensor(equal[:, t, :], logits[:, t, :], fourth.broadcast_to([P, E]), ALU.is_equal))
                nc.vector.tensor_reduce(more[:, t:t + 1], fourths[:, t, :], AX.X, ALU.add)
                link(nc.vector.tensor_tensor_scan(count_eq[:, t, :], ones[:, 0:E], equal[:, t, :], 0.0, ALU.mult, ALU.add))
                link(nc.vector.scalar_tensor_tensor(equal[:, t, :], count_eq[:, t, :], more[:, t:t + 1], equal[:, t, :],
                                                    ALU.is_le, ALU.mult))
                nc.vector.tensor_tensor(chosen[:, t, :], above[:, t, :], equal[:, t, :], ALU.add).then_inc(chosen_ready, 1)

            dve.wait_ge(router_loaded, 32)
            dve.wait_ge(consts, 9)
            for q in range(3):
                add_out(q)
            for half in range(2):
                copy_x1T(0, half)
            choose(0)
            copy_x1T(1, 0)
            add_out(3)
            copy_x1T(1, 1)
            choose(1)
            nc.vector.tensor_tensor(dist_max, logits, top[:, :, 0:1].broadcast_to([P, TT, E]), ALU.subtract).then_inc(centred, 1)
            dve.wait_ge(chosen_ready, TT)
            b = unit("ranks")
            empties(nc.vector.scalar_tensor_tensor(rank[:, :, :].rearrange("p t e -> p (t e)"), chosen.rearrange("p t e -> p (t e)"),
                                                   -UNRANKED, b[:, 0:2 * E], ALU.mult, ALU.add))
            dve.wait_ge(*emptied_at("ranks"))
            pick4 = pick.rearrange("p t (e s) -> p t e s", e=2)
            spread4 = spread.rearrange("p t (e s) -> p t e s", e=2)

            def build_pick(pair):
                ids4 = ids[:, :].unsqueeze(1).unsqueeze(1).broadcast_to([P, TT, 2, SLOTS])
                two = bass.ds(pair * 2, 2)
                nc.vector.tensor_tensor(pick4, ids4, rank[:, :, two].unsqueeze(3).broadcast_to([P, TT, 2, SLOTS]),
                                        ALU.is_equal).then_inc(pick_ready, 1)

            def build_spread(g, pair):
                two = bass.ds(pair * 2, 2)
                dve.wait_ge(pick_ready, g + 1)
                nc.vector.tensor_tensor(spread4, pick4, gate[:, :, two].unsqueeze(3).broadcast_to([P, TT, 2, SLOTS]),
                                        ALU.mult).then_inc(spread_ready, 1)

            def build_rows(pair):
                for e in range(2):
                    ins = nc.vector.tensor_copy(
                        rows[:, :, e, :], ident[:, bass.ds(pair * 8 + 4 * e, NJ)].unsqueeze(2).broadcast_to([P, NJ, SLOTS]))
                ins.then_inc(rows_ready, 1)

            def copy_xg(g, n):
                dve.wait_ge(gather_done, g * 2 + (n + 1))
                nc.vector.tensor_tensor(xgT[:, 4 * n:4 * n + 4, :], turn_banks[n][:, :].rearrange("p (k s) -> p k s", k=4),
                                        g2[:, 4 * n:4 * n + 4].unsqueeze(2).broadcast_to([P, 4, P]), ALU.mult).then_inc(xg_copied, 1)

            def add(q):
                t, n = q // 2, q % 2
                nc.vector.tensor_tensor(acc[:, t, n * CH:(n + 1) * CH], acc[:, t, n * CH:(n + 1) * CH],
                                        scatter_banks[q % 2][:, :], ALU.add).then_inc(added, 1)

            def dve_pass(g, following):
                copy_xg(g, 1)
                for j in range(NJ):
                    dve.wait_ge(up_done, g * UP_LOADS + 2 * (j + 1))
                    if j >= 1:
                        dve.wait_ge(hid_ready, g * NJ + j)
                    pairs = up_banks[j % 2][:, :].rearrange("p (f two) -> p f two", two=2)
                    nc.vector.tensor_scalar(glu, pairs[:, :, 0], LIMIT, None, ALU.min).then_inc(glu_ready, 1)
                    nc.vector.tensor_scalar(lin, pairs[:, :, 1], -LIMIT, LIMIT, ALU.max, ALU.min).then_inc(lin_ready, 1)
                    dve.wait_ge(lin_ready, g * NJ + (j + 1))
                    nc.vector.scalar_tensor_tensor(lin, lin, 1.0, glu, ALU.add, ALU.mult).then_inc(gated_ready, 1)
                    dve.wait_ge(gated_ready, g * NJ + (j + 1))
                    dve.wait_ge(sigmoid_ready, g * NJ + (j + 1))
                    nc.vector.tensor_tensor(hid[:, j * CF:(j + 1) * CF], lin, sig, ALU.mult).then_inc(hid_ready, 1)
                if following:
                    build_pick(g + 1)
                    build_spread(g + 1, g + 1)
                dve.wait_ge(down_done, g * 4 + 4)
                nc.vector.tensor_copy(y[:, CH:2 * CH], down_banks[1][:, :]).then_inc(y1_copied, 1)
                if following:
                    copy_xg(g + 1, 0)
                    build_rows(g + 1)
                for q in range(4):
                    dve.wait_ge(scatter_done, g * 4 + (q + 1))
                    add(q)

            build_pick(0)
            empties(nc.vector.tensor_copy(served[:, :], unit("served")[:, 0:E]))
            dve.wait_ge(expd_ready, 1)
            link(nc.vector.tensor_tensor(expd, expd, chosen, ALU.mult))
            link(nc.vector.tensor_reduce(gsum, expd, AX.X, ALU.add))
            link(nc.vector.reciprocal(ginv, gsum))
            nc.vector.tensor_tensor(gate[:, :, :], expd, ginv.unsqueeze(2).broadcast_to([P, TT, E]), ALU.mult).then_inc(gates_ready, 1)
            dve.wait_ge(gates_ready, 1)
            build_spread(0, 0)
            build_rows(0)
            copy_xg(0, 0)
            n_codes = ROUNDS * PASSES
            code, want, left = extra[:, 0:n_codes], extra[:, 48:48 + n_codes], extra[:, 96:96 + n_codes]
            fuller, best, live = extra[:, 144:160], extra[:, 160:176], extra[:, 176:192]
            count, code_i, round_i = extra[:, 192:193], extra[:, 208:224].bitcast(I32), extra[:, 224:240].bitcast(I32)
            nc.vector.tensor_scalar(code, ids0[:, 0:n_codes], -1.0, n_codes - UNRANKED, ALU.mult, ALU.add)
            dve.wait_ge(*emptied_at("served"))
            both = served[:, :].rearrange("p (g e) -> p g e", e=2)
            link(nc.vector.tensor_tensor(fuller, both[:, :, 0], both[:, :, 1], ALU.max))
            for r in range(ROUNDS):
                part = slice(r * PASSES, (r + 1) * PASSES)
                ins = nc.vector.scalar_tensor_tensor(want[:, part], fuller, float(SLOTS * (r + 1)), code[:, part], ALU.is_gt, ALU.mult)
            link(ins)
            link(nc.vector.max(best[:, 0:8], want))
            link(nc.vector.match_replace(left, best[:, 0:8], want, 0.0))
            link(nc.vector.max(best[:, 8:16], left))
            nc.vector.tensor_scalar(code_i, best, -1.0, float(n_codes), ALU.mult, ALU.add)
            link(nc.vector.tensor_scalar(live, best, 0.5, None, ALU.is_gt))
            link(nc.vector.tensor_reduce(count, live, AX.X, ALU.add))
            nc.vector.tensor_scalar(x_pair[:, :], code_i, PASSES - 1, None, ALU.bitwise_and)
            link(nc.vector.tensor_scalar(round_i, code_i, PASSES.bit_length() - 1, None, ALU.logical_shift_right))
            nc.vector.tensor_scalar(x_off[:, :], round_i, float(SLOTS), float(SLOTS), ALU.mult, ALU.add)
            nc.vector.tensor_copy(n_extra[:, :], count).then_inc(extra_ready, 1)
            dve.wait_ge(extra_ready, 1)
            extras = dve.value_load(n_extra[0:1, 0:1], min_val=0, max_val=LISTED)

            with dve.Fori(0, PASSES - 1) as g:
                dve_pass(g, True)
            dve_pass(PASSES - 1, False)
            with dve.If(extras > 0):
                with dve.Fori(0, extras) as t:
                    pair = dve.value_load(x_pair[0:1, bass.ds(t, 1)], min_val=0, max_val=PASSES - 1)
                    nc.vector.tensor_scalar(ids[:, :], ids0[:, :], x_off[:, bass.ds(t, 1)], None, ALU.add).then_inc(ids_ready, 1)
                    dve.wait_ge(ids_ready, t + 1)
                    build_pick(pair)
                    build_spread(t + PASSES, pair)
                    build_rows(pair)
                    copy_xg(t + PASSES, 0)
                    dve_pass(t + PASSES, False)
            with dve.Else():
                pass
            dve.wait_ge(fin_loaded, 16)
            for t, parts in ((0, [slice(0, D)]), (1, [slice(0, CH), slice(CH, D)])):
                invert_std(t, 2 * TT)
                dve.wait_ge(rstd_ready, 2 * TT + t + 1)
                for part in parts:
                    nc.vector.scalar_tensor_tensor(result[:, t, part], acc[:, t, part], rstd[:, t:t + 1], fin_g[:, part],
                                                   ALU.mult, ALU.mult).then_inc(result_ready, 1)


_INS = ["x", "norm1_g", "w_in", "pool_w", "pool_scale", "w_pool_proj", "sinks", "w_attn_proj", "w_out", "norm2_g",
        "w_router", "b_router", "w_up", "b_up", "w_down", "b_down", "rel_bias", "final_g"]


def kernel(**inputs):
    import concourse.bacc as bacc
    from concourse.bass_utils import run_bass_kernel_spmd

    nc = bacc.Bacc("TRN2", target_bir_lowering=False, num_devices=1)
    arrays, args = {}, []
    for name in _INS:
        a = np.ascontiguousarray(inputs[name])
        arrays[f"in_{name}"] = a
        args.append(nc.dram_tensor(f"in_{name}", a.shape, mybir.dt.from_np(a.dtype), kind="ExternalInput").ap())
    arrays["in_buckets"] = bucket_map()
    args.append(nc.dram_tensor("in_buckets", arrays["in_buckets"].shape, F32, kind="ExternalInput").ap())
    out = nc.dram_tensor("out", (1, SEQ, D), F32, kind="ExternalOutput").ap()
    hybrid_block_kernel(nc, *args, out)
    r = run_bass_kernel_spmd(nc, [arrays], core_ids=[0])
    return r.results[0]["out"]
```
